# Optimizing a Trainium2 kernel written in Bass

```python
import jax, jax.numpy as jnp
from jax import lax
import numpy as np
import jax
import jax.numpy as jnp

D_MODEL = 1024
BATCH = 1
SEQ = 512
DEPTH = 1

CHUNK = 64
POOL_WIDTH = D_MODEL // 2
POOL_GROUPS = 4
POOL_GROUP_DIM = POOL_WIDTH // POOL_GROUPS
POOL_WINDOWS = (2, 4, 8, 16)
CONV_WIDTH = D_MODEL // 2
CONV_K = 31
D_FF = 4 * D_MODEL
IN_COLS = POOL_WIDTH + 2 * CONV_WIDTH + 2 * D_MODEL
EPS = 1e-6


def rmsnorm(x, g):
    xf = x.astype(jnp.float32)
    y = xf * lax.rsqrt(jnp.mean(xf * xf, axis=-1, keepdims=True) + EPS)
    return (y * g.astype(jnp.float32)).astype(x.dtype)

def layernorm(x, g, b):
    xf = x.astype(jnp.float32)
    mu = jnp.mean(xf, axis=-1, keepdims=True)
    var = jnp.mean(jnp.square(xf - mu), axis=-1, keepdims=True)
    y = (xf - mu) * lax.rsqrt(var + EPS)
    return (y * g.astype(jnp.float32) + b.astype(jnp.float32)).astype(x.dtype)

def trailing_mean_minus_self(u, window):
    uf = u.astype(jnp.float32)
    c = jnp.cumsum(uf, axis=1)
    c_prev = jnp.pad(c, ((0, 0), (window, 0), (0, 0)))[:, : u.shape[1], :]
    count = jnp.minimum(jnp.arange(1, u.shape[1] + 1, dtype=jnp.float32), float(window))
    mean = (c - c_prev) / count[None, :, None]
    return (mean - uf).astype(u.dtype)

def pool_mixer(u, pool_w, pool_scale, w_pool_out):
    groups = jnp.split(u, POOL_GROUPS, axis=-1)
    pooled = jnp.stack([trailing_mean_minus_self(g, w) for g, w in zip(groups, POOL_WINDOWS)], axis=2)
    mixed = jnp.einsum('bsgc,gcd->bsgd', pooled, pool_w)
    mixed = mixed.reshape(u.shape) * pool_scale
    return mixed @ w_pool_out

def conformer_conv(glu_in, conv_w, conv_b, ln_g, ln_b, w_conv_out):
    a, gate = jnp.split(glu_in, 2, axis=-1)
    v = a * jax.nn.sigmoid(gate)
    rhs = conv_w.astype(v.dtype)[:, None, :]
    v = lax.conv_general_dilated(v, rhs, window_strides=(1,), padding=[(CONV_K - 1, 0)],
                                 dimension_numbers=('NWC', 'WIO', 'NWC'),
                                 feature_group_count=CONV_WIDTH) + conv_b
    v = layernorm(v, ln_g, ln_b)
    v = jax.nn.silu(v)
    return v @ w_conv_out

def first_inputs(seed: int = 0) -> dict:
    key = jax.random.key(seed)
    ks = jax.random.split(key, 20)
    L, D = DEPTH, D_MODEL
    nrm = lambda k, shape, fan_in: jax.random.normal(k, shape, jnp.float32) * (fan_in ** -0.5)
    gain = lambda k, shape: 1.0 + 0.05 * jax.random.normal(k, shape, jnp.float32)
    return {
        "x": jax.random.normal(ks[0], (BATCH, SEQ, D), jnp.float32),
        "norm_mix_pre": gain(ks[1], (L, D)),
        "w_in": nrm(ks[2], (L, D, IN_COLS), D),
        "pool_w": nrm(ks[3], (L, POOL_GROUPS, POOL_GROUP_DIM, POOL_GROUP_DIM), POOL_GROUP_DIM),
        "pool_scale": gain(ks[4], (L, POOL_WIDTH)),
        "w_pool_out": nrm(ks[5], (L, POOL_WIDTH, D), POOL_WIDTH),
        "conv_w": nrm(ks[6], (L, CONV_K, CONV_WIDTH), CONV_K),
        "conv_b": 0.02 * jax.random.normal(ks[7], (L, CONV_WIDTH), jnp.float32),
        "conv_ln_g": gain(ks[8], (L, CONV_WIDTH)),
        "conv_ln_b": 0.02 * jax.random.normal(ks[9], (L, CONV_WIDTH), jnp.float32),
        "w_conv_out": nrm(ks[10], (L, CONV_WIDTH, D), CONV_WIDTH),
        "w_o": nrm(ks[11], (L, D, D), D),
        "norm_mix_post": gain(ks[12], (L, D)),
        "norm_mlp_pre": gain(ks[13], (L, D)),
        "w_up": nrm(ks[14], (L, D, D_FF), D),
        "w_down": nrm(ks[15], (L, D_FF, D), D_FF),
        "norm_mlp_post": gain(ks[16], (L, D)),
    }

def first_block(x, norm_mix_pre, w_in, pool_w, pool_scale, w_pool_out, conv_w, conv_b,
              conv_ln_g, conv_ln_b, w_conv_out, w_o, norm_mix_post, norm_mlp_pre,
              w_up, w_down, norm_mlp_post):
    for l in range(DEPTH):
        h = rmsnorm(x, norm_mix_pre[l])
        proj = h @ w_in[l]
        u_pool, u_glu, g_a, g_b = jnp.split(
            proj, [POOL_WIDTH, POOL_WIDTH + 2 * CONV_WIDTH, POOL_WIDTH + 2 * CONV_WIDTH + D_MODEL], axis=-1)
        branch_a = pool_mixer(u_pool, pool_w[l], pool_scale[l], w_pool_out[l])
        branch_b = conformer_conv(u_glu, conv_w[l], conv_b[l], conv_ln_g[l], conv_ln_b[l], w_conv_out[l])
        merged = jax.nn.sigmoid(g_a) * branch_a + jax.nn.sigmoid(g_b) * branch_b
        x = x + rmsnorm(merged @ w_o[l], norm_mix_post[l])
        h = rmsnorm(x, norm_mlp_pre[l])
        f = jnp.square(jax.nn.relu(h @ w_up[l])) @ w_down[l]
        x = x + rmsnorm(f, norm_mlp_post[l])
    return x


NSA_HEADS = 8
NSA_KV_GROUPS = 2
NSA_HPG = NSA_HEADS // NSA_KV_GROUPS
NSA_HEAD_DIM = 64
N_NSA_BRANCH = 3
CMP_LEN = 32
CMP_STRIDE = 16
CMP_HIDDEN = 128
SLC_LEN = 64
SLC_TOPK = 16
WINDOW = 512
Q_BLOCK = 128
FORCE_SCORE = 1.0e4

GLA_HEADS = 4
GLA_DK = 64
GLA_DV = 128
GLA_GATE_RANK = 16
GLA_GATE_TAU = 16.0
GLA_CHUNK = 64

ROPE_THETA = 500000.0
ROPE_DIM = NSA_HEAD_DIM // 4

D_FF_2 = (8 * D_MODEL + 3 * 256 - 1) // (3 * 256) * 256

NEG_INF = -1e30

NSA_Q_COLS = NSA_HEADS * NSA_HEAD_DIM
NSA_KV_COLS = N_NSA_BRANCH * 2 * NSA_KV_GROUPS * NSA_HEAD_DIM
NSA_GATE_COLS = NSA_HEADS * N_NSA_BRANCH
GLA_QK_COLS = GLA_HEADS * GLA_DK
GLA_V_COLS = GLA_HEADS * GLA_DV
MERGE_COLS = 2 * D_MODEL
IN_COLS_2 = NSA_Q_COLS + NSA_KV_COLS + NSA_GATE_COLS + 2 * GLA_QK_COLS + 2 * GLA_V_COLS + GLA_GATE_RANK + MERGE_COLS


def rmsnorm_2(x, gain):
    xf = x.astype(jnp.float32)
    y = xf * lax.rsqrt(jnp.mean(xf * xf, axis=-1, keepdims=True) + EPS)
    return (y * gain.astype(jnp.float32)).astype(x.dtype)

def partial_rope(x, pos):
    half = ROPE_DIM // 2
    inv_freq = ROPE_THETA ** (-jnp.arange(half, dtype=jnp.float32) / half)
    ang = pos.astype(jnp.float32)[:, None] * inv_freq[None, :]
    cos = jnp.cos(ang).astype(x.dtype)
    sin = jnp.sin(ang).astype(x.dtype)
    x1 = x[..., :half]
    x2 = x[..., half:ROPE_DIM]
    return jnp.concatenate([x1 * cos - x2 * sin, x2 * cos + x1 * sin, x[..., ROPE_DIM:]], axis=-1)

def masked_softmax(scores, mask):
    p = jax.nn.softmax(jnp.where(mask, scores, NEG_INF), axis=-1)
    return p * mask

def compress_blocks(kv, pe, w1, w2):
    b, g, t, d = kv.shape
    ratio = CMP_LEN // CMP_STRIDE
    n_sub = t // CMP_STRIDE
    n_cmp = n_sub - ratio + 1
    sub = kv.reshape(b, g, n_sub, CMP_STRIDE, d)
    blocks = jnp.concatenate([sub[:, :, r:r + n_cmp] for r in range(ratio)], axis=3)
    blocks = (blocks + pe).reshape(b, g, n_cmp, CMP_LEN * d)
    return jax.nn.silu(blocks @ w1) @ w2

def selection_overlap(n_cmp, n_slc):
    c_start = np.arange(n_cmp)[:, None] * CMP_STRIDE
    s_start = np.arange(n_slc)[None, :] * SLC_LEN
    ov = (c_start < s_start + SLC_LEN) & (c_start + CMP_LEN > s_start)
    return jnp.asarray(ov, dtype=jnp.float32)

def nsa_attention(q, k_cmp, v_cmp, k_slc, v_slc, k_win, v_win, gates):
    b, g, hg, t_len, d = q.shape
    pos = jnp.arange(t_len)
    scale = NSA_HEAD_DIM ** -0.5
    q_rot = partial_rope(q, pos)
    k_slc = partial_rope(k_slc, pos)
    k_win = partial_rope(k_win, pos)
    n_cmp = k_cmp.shape[2]
    cmp_end = jnp.arange(n_cmp) * CMP_STRIDE + CMP_LEN - 1
    n_slc = t_len // SLC_LEN
    topk = min(SLC_TOPK, n_slc)
    overlap = selection_overlap(n_cmp, n_slc)
    kb = k_slc.reshape(b, g, n_slc, SLC_LEN, d)
    vb = v_slc.reshape(b, g, n_slc, SLC_LEN, d)
    kw = jnp.pad(k_win, ((0, 0), (0, 0), (WINDOW, 0), (0, 0)))
    vw = jnp.pad(v_win, ((0, 0), (0, 0), (WINDOW, 0), (0, 0)))
    bi = jnp.arange(b)[:, None, None, None]
    gi = jnp.arange(g)[None, :, None, None]
    blk_ids = jnp.arange(n_slc)

    def query_block(i):
        s = i * Q_BLOCK
        t = s + jnp.arange(Q_BLOCK)
        q_raw = lax.dynamic_slice_in_dim(q, s, Q_BLOCK, axis=3) * scale
        q_pos = lax.dynamic_slice_in_dim(q_rot, s, Q_BLOCK, axis=3) * scale
        sc = jnp.einsum('bghqd,bgnd->bghqn', q_raw, k_cmp, preferred_element_type=jnp.float32)
        p_c = masked_softmax(sc, cmp_end[None, :] <= t[:, None])
        o_c = jnp.einsum('bghqn,bgnd->bghqd', p_c.astype(v_cmp.dtype), v_cmp)
        imp = jnp.einsum('bgqn,nj->bgqj', p_c.sum(axis=2), overlap)
        cur = t[:, None] // SLC_LEN
        valid = blk_ids[None, :] * SLC_LEN <= t[:, None]
        forced = (blk_ids[None, :] == 0) | (blk_ids[None, :] == cur) | (blk_ids[None, :] == cur - 1)
        score = jnp.where(valid, jnp.where(forced, FORCE_SCORE, imp), -jnp.inf)
        top_v, idx = lax.top_k(score, topk)
        ks = kb[bi, gi, idx]
        vs = vb[bi, gi, idx].reshape(b, g, Q_BLOCK, topk * SLC_LEN, d)
        ss = jnp.einsum('bghqd,bgqnld->bghqnl', q_pos, ks, preferred_element_type=jnp.float32)
        ss = ss.reshape(b, g, hg, Q_BLOCK, topk * SLC_LEN)
        tok = idx[..., None] * SLC_LEN + jnp.arange(SLC_LEN)
        m_s = (jnp.isfinite(top_v)[..., None] & (tok <= t[None, None, :, None, None]))
        m_s = m_s.reshape(b, g, 1, Q_BLOCK, topk * SLC_LEN)
        p_s = masked_softmax(ss, m_s)
        o_s = jnp.einsum('bghqm,bgqmd->bghqd', p_s.astype(vs.dtype), vs)
        kwin = lax.dynamic_slice_in_dim(kw, s, WINDOW + Q_BLOCK, axis=2)
        vwin = lax.dynamic_slice_in_dim(vw, s, WINDOW + Q_BLOCK, axis=2)
        kpos = s - WINDOW + jnp.arange(WINDOW + Q_BLOCK)
        dist = t[:, None] - kpos[None, :]
        m_w = (kpos[None, :] >= 0) & (dist >= 0) & (dist < WINDOW)
        sw = jnp.einsum('bghqd,bgkd->bghqk', q_pos, kwin, preferred_element_type=jnp.float32)
        p_w = masked_softmax(sw, m_w)
        o_w = jnp.einsum('bghqk,bgkd->bghqd', p_w.astype(vwin.dtype), vwin)
        gt = lax.dynamic_slice_in_dim(gates, s, Q_BLOCK, axis=3)
        return gt[..., 0:1] * o_c + gt[..., 1:2] * o_s + gt[..., 2:3] * o_w

    out = lax.map(query_block, jnp.arange(t_len // Q_BLOCK))
    return out.transpose(1, 0, 4, 2, 3, 5).reshape(b, t_len, g * hg * d)

def gla_chunked(q, k, v, log_a):
    b, h, t_len, dk = q.shape
    dv = v.shape[-1]
    n_chunk = t_len // GLA_CHUNK

    def to_chunks(a):
        return jnp.moveaxis(a.astype(jnp.float32).reshape(b, h, n_chunk, GLA_CHUNK, a.shape[-1]), 2, 0)

    causal = jnp.tril(jnp.ones((GLA_CHUNK, GLA_CHUNK), dtype=bool))

    def step(state, inp):
        qc, kc, vc, gc = inp
        cum = jnp.cumsum(gc, axis=2)
        last = cum[:, :, -1:, :]
        inter = jnp.einsum('bhtd,bhdv->bhtv', qc * jnp.exp(cum), state)
        diff = jnp.where(causal[:, :, None], cum[:, :, :, None, :] - cum[:, :, None, :, :], -jnp.inf)
        attn = jnp.einsum('bhtd,bhsd,bhtsd->bhts', qc, kc, jnp.exp(diff))
        out = inter + jnp.einsum('bhts,bhsv->bhtv', attn, vc)
        state = jnp.exp(last)[:, :, 0, :, None] * state + jnp.einsum('bhsd,bhsv->bhdv', kc * jnp.exp(last - cum), vc)
        return state, out

    s0 = jnp.zeros((b, h, dk, dv), jnp.float32)
    _, o = lax.scan(step, s0, (to_chunks(q), to_chunks(k), to_chunks(v), to_chunks(log_a)))
    return jnp.moveaxis(o, 0, 2).reshape(b, h, t_len, dv)

def split_in_proj(proj):
    widths = [NSA_Q_COLS, NSA_KV_COLS, NSA_GATE_COLS, GLA_QK_COLS, GLA_QK_COLS, GLA_V_COLS,
              GLA_GATE_RANK, GLA_V_COLS, MERGE_COLS]
    cuts = [int(c) for c in np.cumsum(widths)[:-1]]
    return jnp.split(proj, cuts, axis=-1)

def second_inputs(seed: int = 0) -> dict:
    key = jax.random.key(seed)
    ks = jax.random.split(key, 20)
    L = DEPTH

    def nrm(k, shape, scale):
        return jax.random.normal(k, shape, jnp.float32) * scale

    flat_blk = CMP_LEN * NSA_HEAD_DIM
    return {
        'x': nrm(ks[0], (BATCH, SEQ, D_MODEL), 1.0),
        'norm_mix': 1.0 + nrm(ks[1], (L, D_MODEL), 0.02),
        'w_in': nrm(ks[2], (L, D_MODEL, IN_COLS_2), D_MODEL ** -0.5),
        'cmp_pe_k': nrm(ks[3], (L, CMP_LEN, NSA_HEAD_DIM), 0.1),
        'cmp_pe_v': nrm(ks[4], (L, CMP_LEN, NSA_HEAD_DIM), 0.1),
        'cmp_k_w1': nrm(ks[5], (L, flat_blk, CMP_HIDDEN), flat_blk ** -0.5),
        'cmp_k_w2': nrm(ks[6], (L, CMP_HIDDEN, NSA_HEAD_DIM), CMP_HIDDEN ** -0.5),
        'cmp_v_w1': nrm(ks[7], (L, flat_blk, CMP_HIDDEN), flat_blk ** -0.5),
        'cmp_v_w2': nrm(ks[8], (L, CMP_HIDDEN, NSA_HEAD_DIM), CMP_HIDDEN ** -0.5),
        'gla_gate_w2': nrm(ks[9], (L, GLA_GATE_RANK, GLA_QK_COLS), GLA_GATE_RANK ** -0.5),
        'gla_gate_b': nrm(ks[10], (L, GLA_QK_COLS), 0.1),
        'gla_norm': 1.0 + nrm(ks[11], (L, GLA_DV), 0.02),
        'w_up_nsa': nrm(ks[12], (L, NSA_Q_COLS, D_MODEL), NSA_Q_COLS ** -0.5),
        'w_up_gla': nrm(ks[13], (L, GLA_V_COLS, D_MODEL), GLA_V_COLS ** -0.5),
        'w_out': nrm(ks[14], (L, D_MODEL, D_MODEL), D_MODEL ** -0.5),
        'norm_ffn': 1.0 + nrm(ks[15], (L, D_MODEL), 0.02),
        'w_ffn_gate': nrm(ks[16], (L, D_MODEL, D_FF_2), D_MODEL ** -0.5),
        'w_ffn_up': nrm(ks[17], (L, D_MODEL, D_FF_2), D_MODEL ** -0.5),
        'w_ffn_down': nrm(ks[18], (L, D_FF_2, D_MODEL), D_FF_2 ** -0.5),
        'norm_final': 1.0 + nrm(ks[19], (D_MODEL,), 0.02),
    }

def second_block(x, norm_mix, w_in, cmp_pe_k, cmp_pe_v, cmp_k_w1, cmp_k_w2, cmp_v_w1, cmp_v_w2,
              gla_gate_w2, gla_gate_b, gla_norm, w_up_nsa, w_up_gla, w_out, norm_ffn,
              w_ffn_gate, w_ffn_up, w_ffn_down, norm_final):
    b, t_len, _ = x.shape
    for layer in range(DEPTH):
        h = rmsnorm_2(x, norm_mix[layer])
        proj = h @ w_in[layer]
        q_nsa, kv_nsa, g_nsa, q_gla, k_gla, v_gla, lr_gla, r_gla, g_merge = split_in_proj(proj)
        q_a = q_nsa.reshape(b, t_len, NSA_KV_GROUPS, NSA_HPG, NSA_HEAD_DIM).transpose(0, 2, 3, 1, 4)
        kv = kv_nsa.reshape(b, t_len, 2 * N_NSA_BRANCH, NSA_KV_GROUPS, NSA_HEAD_DIM).transpose(2, 0, 3, 1, 4)
        k_cmp = compress_blocks(kv[0], cmp_pe_k[layer], cmp_k_w1[layer], cmp_k_w2[layer])
        v_cmp = compress_blocks(kv[1], cmp_pe_v[layer], cmp_v_w1[layer], cmp_v_w2[layer])
        gates_a = jax.nn.sigmoid(g_nsa).reshape(b, t_len, NSA_KV_GROUPS, NSA_HPG, N_NSA_BRANCH).transpose(0, 2, 3, 1, 4)
        o_a = nsa_attention(q_a, k_cmp, v_cmp, kv[2], kv[3], kv[4], kv[5], gates_a)
        log_a = jax.nn.log_sigmoid((lr_gla @ gla_gate_w2[layer] + gla_gate_b[layer]).astype(jnp.float32)) / GLA_GATE_TAU
        heads = lambda a, dh: a.reshape(b, t_len, GLA_HEADS, dh).transpose(0, 2, 1, 3)
        o_b = gla_chunked(heads(q_gla * GLA_DK ** -0.5, GLA_DK), heads(k_gla, GLA_DK),
                          heads(v_gla, GLA_DV), heads(log_a, GLA_DK))
        o_b = rmsnorm_2(o_b.transpose(0, 2, 1, 3).astype(x.dtype), gla_norm[layer])
        o_b = (o_b * jax.nn.silu(r_gla.reshape(b, t_len, GLA_HEADS, GLA_DV))).reshape(b, t_len, GLA_V_COLS)
        gate_a, gate_b = jnp.split(jax.nn.sigmoid(g_merge), 2, axis=-1)
        merged = gate_a * (o_a @ w_up_nsa[layer]) + gate_b * (o_b @ w_up_gla[layer])
        x = x + merged @ w_out[layer]
        h = rmsnorm_2(x, norm_ffn[layer])
        x = x + (jax.nn.silu(h @ w_ffn_gate[layer]) * (h @ w_ffn_up[layer])) @ w_ffn_down[layer]
    return rmsnorm_2(x, norm_final)


def setup_inputs(seed=0):
    out = dict(first_inputs(seed))
    for name, value in second_inputs(seed + 1).items():
        if name != "x":
            out[name + "_2"] = value
    return out


def reference(
    x, norm_mix_pre, w_in, pool_w, pool_scale, w_pool_out, conv_w, conv_b, conv_ln_g, conv_ln_b,
    w_conv_out, w_o, norm_mix_post, norm_mlp_pre, w_up, w_down, norm_mlp_post, norm_mix_2,
    w_in_2, cmp_pe_k_2, cmp_pe_v_2, cmp_k_w1_2, cmp_k_w2_2, cmp_v_w1_2, cmp_v_w2_2,
    gla_gate_w2_2, gla_gate_b_2, gla_norm_2, w_up_nsa_2, w_up_gla_2, w_out_2, norm_ffn_2,
    w_ffn_gate_2, w_ffn_up_2, w_ffn_down_2, norm_final_2,
):
    x = first_block(
        x, norm_mix_pre, w_in, pool_w, pool_scale, w_pool_out, conv_w, conv_b, conv_ln_g,
        conv_ln_b, w_conv_out, w_o, norm_mix_post, norm_mlp_pre, w_up, w_down, norm_mlp_post,
    )
    return second_block(
        x, norm_mix_2, w_in_2, cmp_pe_k_2, cmp_pe_v_2, cmp_k_w1_2, cmp_k_w2_2, cmp_v_w1_2,
        cmp_v_w2_2, gla_gate_w2_2, gla_gate_b_2, gla_norm_2, w_up_nsa_2, w_up_gla_2, w_out_2,
        norm_ffn_2, w_ffn_gate_2, w_ffn_up_2, w_ffn_down_2, norm_final_2,
    )


_drawn_inputs = setup_inputs


def setup_inputs(seed=0):
    import zlib

    import numpy as np

    out = dict(_drawn_inputs(seed))
    spreads = {}
    factors = {'conv_b': 2.851,
     'conv_ln_b': 5.95,
     'norm_mix_2': 6.48,
     'cmp_pe_k_2': 8.0,
     'cmp_pe_v_2': 38.038,
     'cmp_k_w1_2': 3.97,
     'cmp_k_w2_2': 4.038,
     'gla_gate_b_2': 5.708,
     'gla_norm_2': 8.0,
     'norm_ffn_2': 17.057}
    for name, (base, spread) in spreads.items():
        noise = np.random.default_rng([zlib.crc32(name.encode()), seed]).standard_normal(out[name].shape)
        drawn = base * np.exp(spread * noise) if base else spread * noise
        out[name] = jnp.asarray(drawn.astype(out[name].dtype))
    for name, factor in factors.items():
        out[name] = (out[name] * factor).astype(out[name].dtype)
    return out
```

```python
import numpy as np
import concourse.bass as bass
from concourse import mybir
from contextlib import ExitStack

P = 128
T = 512
D = 1024
KT = D // P
TT = T // P
POOL_G = 4
CONV_K = 31
CONV_C = 512
CC = CONV_C // P
EPS = 1e-6
SLAB = 256
D_FF = 4096
D_FF2 = 2816
HEADS, HD = 8, 64
N_CMP = 31
GLA_H, GLA_DK, GLA_DV = 4, 64, 128
LEVELS = 7
KB = 1024

C2_Q, C2_KV, C2_GATE, C2_QG, C2_KG, C2_VG, C2_LR, C2_RG, C2_MG = 0, 512, 1280, 1304, 1560, 1816, 2328, 2344, 2856

ROWS = [("norm_mix_pre", 8), ("pool_scale", 4), ("conv_b", 4), ("conv_ln_g", 4), ("conv_ln_b", 4),
        ("norm_mix_post", 8), ("norm_mlp_pre", 8), ("norm_mlp_post", 8), ("norm_mix_2", 8),
        ("norm_ffn_2", 8), ("norm_final_2", 8), ("gla_norm_2", 1), ("gla_gate_b_2", 2),
        ("cmp_pe_k_2", 16), ("cmp_pe_v_2", 16)]
ROW0 = {}
_at = 0
for _name, _n in ROWS:
    ROW0[_name] = _at
    _at += _n
N_ROWS = _at


class Count:

    def __init__(self, sem):
        self.sem, self.n, self.extra = sem, 0, 0

    def inc(self, ins):
        self.n += 1
        ins.then_inc(self.sem, 1)

    def wait(self, eng, back=0):
        eng.wait_ge(self.sem, self.n - back + self.extra)

    def enter(self, i, per):
        self.extra, self.start, self.per = i * per, self.n, per

    def leave(self, times):
        assert self.n - self.start == self.per, (self.n - self.start, self.per)
        self.n, self.extra = self.start + self.per * times, 0


def constants():
    f = np.float32
    ident = np.eye(P, dtype=f)
    recip = np.zeros((P, POOL_G, 16), f)
    for g in range(POOL_G):
        recip[:, g, :] = (f(1) / np.minimum(np.arange(1, 17), 2 << g).astype(f))[None, :]
    half = 8
    inv_freq = f(500000.0) ** (-np.arange(half, dtype=f) / f(half))
    ang = np.arange(T, dtype=f)[None, :] * inv_freq[:, None].astype(f)
    cos, sin = np.ones((P, T), f), np.zeros((P, T), f)
    rot = np.zeros((P, P), f)
    for base in (0, HD):
        for k in range(half):
            cos[base + k] = cos[base + half + k] = np.cos(ang[k])
            sin[base + k] = sin[base + half + k] = np.sin(ang[k])
            rot[base + half + k, base + k] = -1.0
            rot[base + k, base + half + k] = 1.0
    causal = np.where(np.arange(P)[None, :] <= np.arange(P)[:, None], 0.0, -1e30).astype(f)
    cmp_mask = np.full((P, TT, 32), -1e30, f)
    for t in range(TT):
        for n in range(N_CMP):
            cmp_mask[:, t, n] = np.where(16 * n + 31 <= t * P + np.arange(P), 0.0, -1e30)
    level = np.zeros((P, LEVELS + 1, P), f)
    s, t = np.arange(P)[:, None], np.arange(P)[None, :]
    for l in range(LEVELS):
        h = 64 >> l
        level[:, l] = ((s // (2 * h) == t // (2 * h)) & (s % (2 * h) < h) & (t % (2 * h) >= h))
    level[:, LEVELS] = s == t
    reset = np.broadcast_to((np.arange(T) % P != 0).astype(f), (P, T))
    return {"c_ident": ident, "c_recip": recip.reshape(P, -1), "c_cos": cos, "c_sin": sin, "c_rot": rot,
            "c_causal": causal, "c_cmp_mask": cmp_mask.reshape(P, -1), "c_level": level.reshape(P, -1),
            "c_reset": np.ascontiguousarray(reset)}


def build(nc, a, out):
    f32, f32r, bf16 = mybir.dt.float32, mybir.dt.float32r, mybir.dt.bfloat16
    ALU, ACT, AX = mybir.AluOpType, mybir.ActivationFunctionType, mybir.AxisListType
    ADD, SUB, MUL, MAX = ALU.add, ALU.subtract, ALU.mult, ALU.max

    def at(name, shape, dt, kb):
        return nc.alloc_sbuf_tensor_at(name, [P] + shape, dt, offset=16512 + int(kb * KB))

    def f(ap):
        return ap.bitcast(f32)

    XT = at("x_T", [KT, T], f32, 0)
    HHI, HLO = at("h_hi", [KT, T], f32r, 16), at("h_lo", [KT, T], f32r, 32)
    RAW = [at(f"w_raw{i}", [KT, SLAB], f32, 48 + 8 * i) for i in range(2)]
    WHI = [at(f"w_hi{i}", [KT, SLAB], f32r, 64 + 8 * i) for i in range(2)]
    WLO = [at(f"w_lo{i}", [KT, SLAB], f32r, 80 + 8 * i) for i in range(2)]
    CB = 96
    IDENT = at("ident", [P], f32, CB)
    INV = {n: at(f"inv{n}", [P], f32, CB + 0.5 * (1 + j)) for j, n in enumerate((1024, 512, 128))}
    PV, CW = at("param_cols", [P], f32, CB + 2), at("conv_cols", [P], f32, CB + 2.5)
    RECIP = at("recip", [POOL_G, 16], f32, CB + 3)
    EPSB = at("eps", [1], f32, CB + 3.25)
    TMP16 = at("pool_head", [16], f32, CB + 3.375)
    ROT = at("rot", [P], f32, CB + 3.5)
    CAUS32, CAUSB = at("causal32", [P], f32, CB + 4), at("causal", [P], bf16, CB + 4.5)
    IDENTB = at("ident_b", [P], bf16, CB + 4.75)
    CMPM32, CMPMB = at("cmp_mask32", [TT, 32], f32, CB + 5), at("cmp_mask", [TT, 32], bf16, CB + 5.5)
    ROWS_T, CROWS_T = at("param_rows", [P], f32, CB + 6), at("conv_rows", [P], f32, CB + 6.5)
    W2G = at("gla_w2", [GLA_H * GLA_DK], f32, CB + 7)
    SB = 105
    SQ = [at(f"sq{i}", [T], f32, SB + 2 * i) for i in range(2)]
    HS = [at(f"h_now{i}", [T], f32, SB + 4 + 2 * i) for i in range(2)]
    SQA, RS, RSTD = (at(n, [T], f32, SB + 8 + 2 * j) for j, n in enumerate(("sq_sum", "root", "rstd")))
    R1 = 119.5
    GT = at("gate_tanh", [2 * KT, T], f32, R1)
    XTOK = at("x_tok", [TT, D], f32, R1)
    VP = at("v_padded", [CC, 30 + T], f32, R1 + 32)
    CV = at("conv_out", [CC, T], f32, R1 + 40.5)
    PHI, PLO = at("pool_hi", [POOL_G, T], f32r, R1 + 48.5), at("pool_lo", [POOL_G, T], f32r, R1 + 56.5)
    CHI, CLO = at("conv_hi", [CC, T], f32r, R1 + 64.5), at("conv_lo", [CC, T], f32r, R1 + 72.5)
    PLD = at("pooled", [POOL_G, T], f32, R1 + 64.5)
    UP = at("u_padded", [16 + T], f32, R1 + 72.5)
    S2 = [at(f"window_sum{i}", [16 + T], f32, R1 + 74.75 + 2.25 * i) for i in range(2)]
    POOLW = at("pool_w_sb", [POOL_G, P], f32, R1 + 80.5)
    SG = [at(f"glu_tanh{i}", [T], f32, SB + 4 + 2 * i) for i in range(2)]
    Y = at("y_T", [KT, T], f32, R1 + 66)
    FHI = [at(f"f_hi{i}", [KT, T], f32r, R1 + 32 * i) for i in range(2)]
    FLO = [at(f"f_lo{i}", [KT, T], f32r, R1 + 16 + 32 * i) for i in range(2)]
    RL = [at(f"relu{i}", [T], f32, SB + 4 + 2 * i) for i in range(2)]
    FF = [at(f"f_now{i}", [T], f32, SB + 2 * i) for i in range(2)]

    G = [nc.alloc_psum_tensor(f"gemm{i}", [P, T], f32) for i in range(4)]
    M = [nc.alloc_psum_tensor(f"misc{i}", [P, T], f32) for i in range(4)]

    ctx = ExitStack()
    sems = {}

    def S(name):
        if name not in sems:
            sems[name] = ctx.enter_context(nc.semaphore(name))
        return sems[name]

    raw_ready = [S("raw_ready0"), S("raw_ready1")]
    evac = [S(f"evacuated{i}") for i in range(4)]

    PH, s_at, b_at = {}, 0, 0
    for name, n, bps in [("in", 14, 2), ("branch", 4, 4), ("wo", 4, 2)] + \
            [("up0", 4, 2), ("up1", 4, 2), ("down0", 4, 2), ("up2", 4, 2), ("down1", 4, 2), ("up3", 4, 2),
             ("down2", 4, 2), ("down3", 4, 2)] + \
            [("small", 1, 1), ("gla", 6, 2), ("nsa", 5, 2), ("merge", 8, 2), ("branch2", 4, 4), ("wout", 4, 2),
             ("fup0", 8, 2), ("fup1", 8, 2), ("fdown0", 4, 2), ("fup2", 6, 2), ("fdown1", 4, 2), ("fdown2", 4, 2)]:
        PH[name] = (s_at, n, b_at, bps)
        s_at, b_at = s_at + n, b_at + n * bps
    N_SLABS = s_at
    BLOCKS_BEFORE = []
    for s0, n, b0, bps in PH.values():
        BLOCKS_BEFORE += [b0 + j * bps for j in range(n)]
    BLOCKS_BEFORE.append(b_at)

    def evac_at(m, i=0, per=0):
        return evac[m % 4], m // 4 + 3 + i * (per // 4)

    def col(name, j=0, h=False):
        return PV[:, ROW0[name] + j:ROW0[name] + j + 1]

    def tiles(ap):
        return ap.rearrange("(k p) c -> p k c", p=P)

    w_in, w_po, w_co, w_o = (tiles(a[n][0]) for n in ("w_in", "w_pool_out", "w_conv_out", "w_o"))
    w_up, w_down = tiles(a["w_up"][0]), tiles(a["w_down"][0])
    ds = bass.ds
    block = ctx.enter_context(nc.Block())
    CONST_DMAS = 8

    ONEB, GTH, GATES = at("one", [1], f32, CB + 8), at("gate_tanh_small", [TT, 24], f32, CB + 8.125), at("gates", [TT, 24], f32, CB + 8.5)
    EL = at("gla_chunk_decay", [2, TT], f32, CB + 8.875)
    W1 = [at(f"cmp_w1_{i}", [16, P], f32, R1 + 8 * i) for i in range(2)]
    A = at("gla_attn", [GLA_H, T], f32, R1 + 16)
    OSB = at("gla_out", [GLA_H, T], f32, R1 + 16)
    RG = at("gla_gate", [GLA_H, T], f32, R1 + 24)
    QG, KG = at("q_gla", [2, T], f32, R1 + 32), at("k_gla", [2, T], f32, R1 + 36)
    VG = at("v_gla", [TT, GLA_H, GLA_DV], f32, R1 + 40)
    CUM, SMALL = at("log_decay", [2, T], f32, R1 + 48), at("lr_and_gates", [T], f32, R1 + 52)
    LEVM = at("level_masks", [LEVELS + 1, P], mybir.dt.uint8, R1 + 54)
    LEV32 = at("level_masks32", [LEVELS + 1, P], f32, R1 + 55)
    QL, KL = at("q_level", [2, T], f32, R1 + 55), at("k_level", [2, T], f32, R1 + 59)
    RESET = at("chunk_start", [T], f32, R1 + 59)
    RS4 = at("gla_roots", [GLA_H, T], f32, R1 + 55)
    ST = at("gla_state", [2, 3, GLA_DV], f32, R1 + 63)
    KTOK = at("k_tokens", [TT, GLA_H * GLA_DK], f32, SB + 4)
    VS = [at(f"v_stage{i}", [T], f32, SB + 10 + 2 * i) for i in range(2)]
    QR, QT = at("q_raw", [4, T], f32, R1 + 66), at("q_rope", [4, T], f32, R1 + 32)
    KR, VT = at("k_rope", [2, T], f32, R1 + 74), at("v_tokens", [2, TT, P], f32, R1 + 78)
    RAWC = at("kv_cmp_raw", [2, T], f32, R1 + 82)
    COS, SIN = at("cos", [T], f32, SB + 8), at("sin", [T], f32, R1 + 86)
    OBHI, OBLO = at("ob_hi", [4, T], f32r, R1 + 40), at("ob_lo", [4, T], f32r, R1 + 48)
    Z = at("cmp_windows", [4, T], f32, R1 + 56)
    OA = at("oa_tokens", [TT, HEADS * HD], f32, R1 + 56)
    VBD = at("v_cmp_blocks", [2, 4 * HD], f32, R1 + 82)
    W2 = [at(f"cmp_w2_{i}", [HD], f32, R1 + 64 + 0.25 * i) for i in range(2)]
    HX = [at(f"cmp_hidden{i}", [2 * 32], f32, R1 + 64.5 + 0.25 * i) for i in range(2)]
    HT = [at(f"cmp_tanh{i}", [2 * 32], f32, R1 + 65 + 0.25 * i) for i in range(2)]
    HB = at("cmp_bias", [2], f32, R1 + 65.5)
    KC = at("k_cmp", [32], f32, R1 + 65.625)
    KNOW = at("k_now", [T], f32, R1 + 84)
    PC, PCT = at("p_cmp", [TT, HEADS, 32], f32, SB), at("p_cmp_T", [2 * TT, P], f32, SB + 4)
    PB = [at(f"probs{i}", [2, T], f32, SB + 4 * i) for i in range(2)]
    PT = [at(f"probs_T{i}", [T], f32, SB + 8 + 2 * i) for i in range(2)]
    OTMP = at("o_scaled", [T], f32, SB + 12)
    MXC, SMC, FC = (at(n, [TT * HEADS], f32, R1 + 86 + 0.125 * j) for j, n in enumerate(("cmp_max", "cmp_sum", "cmp_factor")))
    NM = [at(f"row_max{i}", [2], f32, R1 + 86.5 + 0.0625 * i) for i in range(2)]
    NG = [at(f"neg_max{i}", [2], f32, R1 + 86.625 + 0.0625 * i) for i in range(2)]
    SUM = [at(f"row_sum{i}", [HEADS], f32, R1 + 86.75 + 0.0625 * i) for i in range(2)]
    FS = at("o_factor", [HEADS], f32, R1 + 86.875)
    OAHI, OALO = at("oa_hi", [4, T], f32r, R1 + 66), at("oa_lo", [4, T], f32r, R1 + 32)
    FG = [at(f"ffn_now{i}", [T], f32, R1 + 82 + 2 * i) for i in range(2)]
    OTK = at("out_tokens", [TT, D], f32, R1)

    read = [S(f"misc_read{i}") for i in range(4)]
    H2, F2 = 7 * KT, 4 * KT

    @block.sync
    def _(sp):
        for t in range(TT):
            sp.dma_start(XTOK[:, t, :], a["x"][0, t * P:(t + 1) * P, :]).then_inc(S("x_loaded"), 16)

        def load(s, par, pieces, first=False, quarter=False):
            if not first:
                sp.wait_ge(S("lo_done"), s - 1)
            for dst, src in pieces:
                sp.dma_start(dst, src).then_inc(raw_ready[par], 16)

        def halves(par, w, k0, c0, kts=KT):
            h = kts // 2
            return [(RAW[par][:, 0:h, :], w[:, k0:k0 + h, ds(c0, SLAB)]),
                    (RAW[par][:, h:kts, :], w[:, k0 + h:k0 + kts, ds(c0, SLAB)])]

        def run(name, w, k0=0, c0=0, kts=KT):
            s0, n = PH[name][0:2]
            with sp.Fori(0, n // 2) as i:
                for j in range(2):
                    load(s0 + j + 2 * i, (s0 + j) % 2, halves((s0 + j) % 2, w, k0, c0 + SLAB * j + 2 * SLAB * i, kts))

        for c in range(CC):
            par = c % 2
            load(c, par, [(RAW[par][:, :, 0:P], w_in[:, :, 512 + c * P:512 + (c + 1) * P]),
                          (RAW[par][:, :, P:SLAB], w_in[:, :, 1024 + c * P:1024 + (c + 1) * P])], first=c < 2)
        for j in range(2):
            load(4 + j, j, halves(j, w_in, 0, SLAB * j))
        with sp.Fori(0, 4) as i:
            for j in range(2):
                load(6 + j + 2 * i, j, halves(j, w_in, 0, 1536 + SLAB * j + 2 * SLAB * i))
        s0 = PH["branch"][0]
        with sp.Fori(0, 2) as i:
            for j in range(2):
                load(s0 + j + 2 * i, j, [(RAW[j][:, 0:4, :], w_po[:, :, ds(SLAB * j + 2 * SLAB * i, SLAB)]),
                                         (RAW[j][:, 4:8, :], w_co[:, :, ds(SLAB * j + 2 * SLAB * i, SLAB)])])
        run("wo", w_o)
        for ch in range(4):
            run(f"up{ch}", w_up, c0=1024 * ch)
            if ch:
                run(f"down{ch - 1}", w_down, k0=KT * (ch - 1))
        run("down3", w_down, k0=KT * 3)
        w_2 = tiles(a["w_in_2"][0])
        s0 = PH["small"][0]
        load(s0, 0, [(RAW[0][:, :, 0:32], w_2[:, :, C2_LR:C2_LR + 32]),
                     (RAW[0][:, :, 32:P], w_2[:, :, C2_GATE:C2_GATE + 96])])
        for j, c0 in enumerate((C2_QG, C2_KG, C2_VG, C2_VG + SLAB, C2_RG, C2_RG + SLAB,
                                C2_KV, C2_KV + SLAB, C2_KV + 2 * SLAB)):
            load(s0 + 1 + j, (1 + j) % 2, halves((1 + j) % 2, w_2, 0, c0))
        for j in range(2):
            par = j % 2
            load(s0 + 10 + j, par, [(RAW[par][:, :, :].rearrange("p k (b g d) -> p k b g d", b=2, g=2)[:, :, b, g, :],
                                     w_2[:, :, g * 4 * HD + (2 * j + b) * HD:g * 4 * HD + (2 * j + b + 1) * HD])
                                    for b in range(2) for g in range(2)], quarter=True)
        run("merge", w_2, c0=C2_MG)
        w_ua, w_ub = tiles(a["w_up_nsa_2"][0]), tiles(a["w_up_gla_2"][0])
        s0 = PH["branch2"][0]
        with sp.Fori(0, 2) as i:
            for j in range(2):
                load(s0 + j + 2 * i, j, [(RAW[j][:, 0:4, :], w_ua[:, :, ds(SLAB * j + 2 * SLAB * i, SLAB)]),
                                         (RAW[j][:, 4:8, :], w_ub[:, :, ds(SLAB * j + 2 * SLAB * i, SLAB)])])
        run("wout", tiles(a["w_out_2"][0]))
        w_g, w_u, w_d = (tiles(a[n][0]) for n in ("w_ffn_gate_2", "w_ffn_up_2", "w_ffn_down_2"))

        def gate_up(name, c0):
            s0, n = PH[name][0:2]
            with sp.Fori(0, n // 2) as i:
                for j, w in enumerate((w_g, w_u)):
                    load(s0 + j + 2 * i, (s0 + j) % 2, halves((s0 + j) % 2, w, 0, c0 + SLAB * i))

        gate_up("fup0", 0)
        gate_up("fup1", 1024)
        run("fdown0", w_d)
        gate_up("fup2", 2048)
        run("fdown1", w_d, k0=KT)
        run("fdown2", w_d, k0=2 * KT, kts=6)
        for k in range(KT):
            sp.wait_ge(S("out_ready"), k + 1)
            sp.dma_start(out[0].rearrange("(t p) c -> p t c", p=P)[:, :, k * P:(k + 1) * P],
                         OTK[:, :, k * P:(k + 1) * P]).then_inc(S("stored"), 16)
        sp.wait_ge(S("stored"), 16 * KT)

    @block.tensor
    def _(pe):
        norms = [0]
        squares = Count(S("sq_used"))

        def gemm(bank, free, par, kts, col0, hi, lo, ready=None):
            pe.wait_ge(*free)
            first = True
            for n, kt in enumerate(kts):
                if ready:
                    ready(n)
                for w, x in ((WHI, hi), (WHI, lo), (WLO, hi)):
                    last = n == len(kts) - 1 and w is WLO
                    mm = nc.tensor.matmul(bank[:], w[par][:, kt, col0:col0 + P], x(n), start=first, stop=last)
                    first = False
            mm.then_inc(S("block_full"), 1)

        def slab(s, par, m, i, per, hi, lo, kts=range(KT), ready=None, blocks=2):
            pe.wait_ge(S("lo_done"), s + 1)
            for b in range(blocks):
                gemm(G[(m + b) % 4], (evac[(m + b) % 4], (m + b) // 4 + 2 + i * (per // 4)), par, kts, P * b, hi, lo,
                     ready if b == 0 else None)

        def h(t):
            return lambda n: t[:, n, :]

        def h_ready(base):
            return lambda n: pe.wait_ge(S("hlo_ready"), base + n + 1)

        def run(name, hi, lo, kts=range(KT), ready=None, lo_slab=0, slabs=None):
            s0, n, b0, bps = PH[name]
            n = slabs or n
            s0, b0 = s0 + lo_slab, b0 + lo_slab * bps
            if n == 2:
                for j in range(2):
                    slab(s0 + j, (s0 + j) % 2, b0 + j * bps, 0, 0, hi, lo, kts, ready)
                return
            with pe.Fori(0, n // 2) as i:
                for j in range(2):
                    slab(s0 + j + 2 * i, (s0 + j) % 2, b0 + j * bps, i, 2 * bps, hi, lo, kts, ready)

        def mean_of_tiles(width, count, bank, ready_sem, base, done_sem, src=None):
            for k in range(count):
                pe.wait_ge(ready_sem, base + k + 1)
                x = src[:, k, :] if src is not None else SQ[k % 2][:]
                mm = nc.tensor.matmul(bank[:], INV[width][:], x, start=k == 0, stop=k == count - 1)
                if k < count - 1:
                    squares.inc(mm)
            mm.then_inc(done_sem, 1)

        def mean_of_sum(bank, ready_at):
            pe.wait_ge(S("sq_added"), ready_at)
            nc.tensor.matmul(bank[:], INV[1024][:], SQA[:], start=True, stop=True).then_inc(S("mean_ready"), 1)

        pe.wait_ge(S("consts_loaded"), CONST_DMAS * 16)
        pe.wait_ge(S("x_loaded"), 16 * TT)
        for k in range(KT):
            if k >= 4:
                pe.wait_ge(evac[k % 4], 1)
            for t in range(TT):
                mm = nc.tensor.transpose(G[k % 4][:, t * P:(t + 1) * P], XTOK[:, t, k * P:(k + 1) * P], IDENT[:])
            mm.then_inc(S("x_transposed"), 1)
        nc.tensor.transpose(M[1][:, 0:N_ROWS], ROWS_T[0:N_ROWS, :], IDENT[0:N_ROWS, 0:N_ROWS]).then_inc(S("rows_transposed"), 1)
        nc.tensor.transpose(M[2][:, 0:CONV_K * CC], CROWS_T[0:CONV_K * CC, :], IDENT[0:CONV_K * CC, 0:CONV_K * CC]).then_inc(S("rows_transposed"), 1)
        pe.wait_ge(S("inv_ready"), 1)
        mean_of_tiles(1024, KT, M[0], S("sq_ready"), 0, S("mean_ready"))
        pe.wait_ge(S("cols_ready"), 2)

        run("in", h(HHI), h(HLO), ready=h_ready(0), slabs=6)
        run("in", h(HHI), h(HLO), lo_slab=6, slabs=4)
        pe.wait_ge(S("pool_w_loaded"), 16)
        for g in range(POOL_G):
            pe.wait_ge(S("pooled_ready"), g + 1)
            nc.tensor.matmul(M[g][:], POOLW[:, g, :], PLD[:, g, :], start=True, stop=True).then_inc(S("mixed"), 1)
        run("in", h(HHI), h(HLO), lo_slab=10, slabs=2)
        pe.wait_ge(S("pool_lo_ready"), POOL_G)
        mean_of_tiles(512, CC, M[0], S("conv_ready"), 0, S("ln_mean"), src=CV)
        run("in", h(HHI), h(HLO), lo_slab=12, slabs=2)
        mean_of_tiles(512, CC, M[1], S("lsq_ready"), 0, S("ln_var"), src=PLD)
        s0, _, b0, _ = PH["branch"]
        pe.wait_ge(S("clo_ready"), CC)
        with pe.Fori(0, 2) as i:
            for j in range(2):
                pe.wait_ge(S("lo_done"), s0 + j + 1 + 2 * i)
                for b in range(4):
                    hi, lo = ((PHI, PLO), (CHI, CLO))[b % 2]
                    m = b0 + 4 * j + b
                    gemm(G[m % 4], (evac[m % 4], m // 4 + 2 + 2 * i), j, range(4 * (b % 2), 4 * (b % 2) + 4),
                         P * (b // 2), h(hi), h(lo))
        hlo = KT
        run("wo", h(HHI), h(HLO), ready=h_ready(hlo))
        mean_of_sum(M[0], KT + 1)
        mean_of_tiles(1024, KT, M[0], S("sq_ready"), KT, S("mean_ready"))
        hlo += KT
        for ch in range(4):
            run(f"up{ch}", h(HHI), h(HLO), ready=h_ready(hlo) if ch == 0 else None)
            if ch:
                c = ch - 1
                run(f"down{c}", h(FHI[c % 2]), h(FLO[c % 2]), ready=h_ready(hlo + KT * (c + 1)))
        run("down3", h(FHI[1]), h(FLO[1]), ready=h_ready(hlo + KT * 4))
        mean_of_sum(M[0], 2 * (KT + 1))
        mean_of_tiles(1024, KT, M[0], S("sq_ready"), 2 * KT, S("mean_ready"))
        misc = [Count(x) for x in read]

        def take(b):
            if misc[b].n or misc[b].extra:
                misc[b].wait(pe)
            misc[b].n += 1
            return M[b]

        hlo = H2
        s0, _, m0, _ = PH["small"]
        ready2 = h_ready(hlo)

        def plain(j, blocks=2, m=None):
            s = s0 + j
            slab(s, s % 2, BLOCKS_BEFORE[s], 0, 0, h(HHI), h(HLO), ready=ready2 if j == 0 else None, blocks=blocks)

        plain(0, 1)
        plain(1)
        pe.wait_ge(*evac_at(m0))
        b1 = take(1)
        for t in range(TT):
            mm = nc.tensor.transpose(b1[:, t * 64:t * 64 + 64], SMALL[0:64, t * P:(t + 1) * P], IDENT[0:64, 0:64])
        mm.then_inc(S("gates_T"), 1)
        for j in range(2):
            nc.tensor.matmul(take(2 + j)[:], W2G[0:16, j * P:(j + 1) * P], SMALL[0:16, :], start=True, stop=True).then_inc(S("decay_in"), 1)
        plain(2)
        plain(3)

        def to_tokens(src, bank, sem):
            for t in range(TT):
                mm = nc.tensor.transpose(bank[:, t * P:(t + 1) * P], src[:, t * P:(t + 1) * P], IDENT[:])
            mm.then_inc(S(sem), 1)

        def v_head(hd):
            pe.wait_ge(*evac_at(BLOCKS_BEFORE[s0 + 3] + hd))
            to_tokens(VS[hd % 2], take(hd), "v_T")

        plain(4)
        v_head(0)
        v_head(1)
        plain(5)
        v_head(2)
        v_head(3)
        plain(6)

        def level(l):
            ql, kl = (QL, KL) if l < LEVELS else (QG, KG)
            if l < LEVELS:
                pe.wait_ge(S("ql_ready"), 2 * (l + 1))
                pe.wait_ge(S("kl_ready"), 2 * (l + 1))
            for hd in range(GLA_H):
                bank, pp = take(hd), GLA_DK * (hd % 2)
                for c in range(TT):
                    mm = nc.tensor.matmul(bank[:, c * P:(c + 1) * P], kl[pp:pp + GLA_DK, hd // 2, c * P:(c + 1) * P],
                                          ql[pp:pp + GLA_DK, hd // 2, c * P:(c + 1) * P], start=True, stop=True)
                mm.then_inc(S("level_full"), 1)

        def half(j, b):
            s = s0 + j
            m = BLOCKS_BEFORE[s] + b
            if b == 0:
                pe.wait_ge(S("lo_done"), s + 1)
            gemm(G[m % 4], (evac[m % 4], m // 4 + 2), s % 2, range(KT), P * b, h(HHI), h(HLO))

        def v_branch(i):
            pe.wait_ge(*evac_at(BLOCKS_BEFORE[s0 + 7] + 3 + 2 * i))
            to_tokens(VS[i], take(0), "vb_T")

        for k in range(10):
            half(7 + k // 2, k % 2)
            if k == 4:
                v_branch(0)
            if k == 6:
                v_branch(1)
            if k <= LEVELS:
                level(k)
        pe.wait_ge(S("kl_ready"), 2 * LEVELS + 2)
        for j in range(2):
            to_tokens(KL[:, j, :], take(j), "k_T")
        misc[0].wait(pe)
        misc[1].wait(pe)
        for j in range(2):
            bank = take(2 + j)
            for c in range(3):
                for q in range(2):
                    hd = 2 * j + q
                    mm = nc.tensor.matmul(bank[q * 64:q * 64 + 64, c * P:(c + 1) * P], KTOK[:, c, hd * 64:hd * 64 + 64],
                                          VG[:, c, hd, :], start=True, stop=True)
            mm.then_inc(S("update_full"), 1)
        misc[2].wait(pe)
        misc[3].wait(pe)
        pe.wait_ge(S("ql_ready"), 2 * LEVELS + 2)
        for hd in range(GLA_H):
            bank, pp = take(hd), GLA_DK * (hd % 2)
            for c in range(TT):
                cs = slice(c * P, (c + 1) * P)
                mm = nc.tensor.matmul(bank[:, cs], VG[:, c, hd, :], A[:, hd, cs], start=True, stop=c == 0)
                if c:
                    mm = nc.tensor.matmul(bank[:, cs], ST[pp:pp + 64, hd // 2, c - 1, :], QL[pp:pp + 64, hd // 2, cs],
                                          start=False, stop=True)
            mm.then_inc(S("gla_out_full"), 1)
        for hd in range(GLA_H):
            pe.wait_ge(S("gla_sq_ready"), hd + 1)
            nc.tensor.matmul(take(hd)[:], INV[128][:], SQ[hd % 2][:], start=True, stop=True).then_inc(S("gla_mean"), 1)
        pe.wait_ge(*evac_at(BLOCKS_BEFORE[s0 + 11] + 1))
        for n in range(6):
            x = KR[:, n, :] if n < 2 else QR[:, n - 2, :]
            nc.tensor.matmul(take(n % 4)[:], ROT[:], x, start=True, stop=True).then_inc(S("rotated"), 1)
        pe.wait_ge(S("cmp_loaded"), 16 * 4)
        pe.wait_ge(S("windows_a"), 4)
        pe.wait_ge(S("windows_b"), 4)
        for kv in range(2):
            bank = take(2 + kv)
            row = ROW0[("cmp_pe_k_2", "cmp_pe_v_2")[kv]]
            for j in range(16):
                nc.tensor.matmul(bank[:, 64:65], W1[kv][:, j, :], PV[:, row + j:row + j + 1], start=j == 0, stop=j == 15)
            for g in range(2):
                for j in range(16):
                    mm = nc.tensor.matmul(bank[:, 32 * g:32 * g + N_CMP], W1[kv][:, j, :],
                                          Z[:, 2 * kv + g, 2 * j:2 * j + 16 * (N_CMP - 1) + 1:16], start=j == 0, stop=j == 15)
            mm.then_inc(S("hidden_full"), 1)
        pe.wait_ge(S("hidden_ready"), 1)
        bank = take(0)
        for g in range(2):
            mm = nc.tensor.matmul(bank[64 * g:64 * g + 64, 0:N_CMP], W2[0][:], HX[0][:, 32 * g:32 * g + N_CMP], start=True, stop=True)
        mm.then_inc(S("kc_full"), 1)
        pe.wait_ge(S("hidden_ready"), 2)
        bank = take(1)
        for g in range(2):
            mm = nc.tensor.matmul(bank[0:32, 64 * g:64 * g + 64], HX[1][:, 32 * g:32 * g + 32], W2[1][:], start=True, stop=True)
        mm.then_inc(S("vc_full"), 1)
        misc[0].wait(pe)
        pe.wait_ge(S("masks_ready"), 1)
        for g in range(2):
            bank = take(2 + g)
            nc.tensor.matmul(bank[:].rearrange("p (t h n) -> p t h n", h=4, n=32), IDENTB[:],
                             CMPMB[:].unsqueeze(2).broadcast_to([P, TT, 4, 32]), start=True, stop=False)
            for t in range(TT):
                for q in range(4):
                    o = P * t + 32 * q
                    mm = nc.tensor.matmul(bank[:, o:o + N_CMP], QR[64 * g:64 * g + 64, q, t * P:(t + 1) * P],
                                          KC[64 * g:64 * g + 64, 0:N_CMP], start=False, stop=t == TT - 1 and q == 3)
            mm.then_inc(S("cmp_scores"), 1)
        pe.wait_ge(S("cmp_probs"), 2)
        for t in range(TT):
            bank = take(t // 2) if t % 2 == 0 else bank
            for g in range(2):
                mm = nc.tensor.transpose(bank[:, (2 * (t % 2) + g) * P:(2 * (t % 2) + g + 1) * P],
                                         PC[:].rearrange("p t h n -> p t (h n)")[:, t, P * g:P * (g + 1)], IDENT[:])
            mm.then_inc(S("probs_T_full"), 1)
        for t in range(TT):
            if t % 2 == 0:
                misc[t // 2].wait(pe)
            bank = take((2 + t) % 4)
            for g in range(2):
                mm = nc.tensor.matmul(bank[:, 256 * g:256 * g + 256], PCT[:, 2 * t + g, :], VBD[:, g, :], start=True, stop=True)
            mm.then_inc(S("cmp_out_full"), 1)
        sM, _, mM, _ = PH["merge"]

        def gate_matmuls(i, first, count):
            for x in range(first, first + count):
                bl, kt, n = x // 24, x % 24 // 3, x % 3
                m = mM + bl
                if x % 48 == 0:
                    pe.wait_ge(S("lo_done"), sM + bl // 2 + 1 + 4 * i)
                if x % 24 == 0:
                    pe.wait_ge(evac[m % 4], m // 4 + 2 + 2 * i)
                w, y = ((WHI, HHI), (WHI, HLO), (WLO, HHI))[n]
                mm = nc.tensor.matmul(G[m % 4][:], w[bl // 2 % 2][:, kt, P * (bl % 2):P * (bl % 2) + P], y[:, kt, :],
                                      start=kt == 0 and n == 0, stop=kt == KT - 1 and n == 2)
                if x % 24 == 23:
                    mm.then_inc(S("block_full"), 1)

        pe.wait_ge(S("ropes_ready"), 6)
        with pe.Fori(0, 2) as i:
            per = (16, 16, 32, 4)
            for b in range(4):
                misc[b].enter(i, per[b])
            pe.wait_ge(S("keys_moved"), i + 1)
            for t in range(TT):
                out_bank = take(3)
                w = t * P
                for q in range(4):
                    for g in range(2):
                        bank = take(g)
                        qs = QT[64 * g:64 * g + 64, q, w:w + P]
                        kr = KNOW[64 * g:64 * g + 64, :]
                        nc.tensor.matmul(bank[:, w:w + P], IDENTB[:], CAUSB[:], start=True, stop=False)
                        if t:
                            nc.tensor.matmul(bank[:, 0:w], qs, kr[:, 0:w], start=False, stop=False)
                        nc.tensor.matmul(bank[:, w:w + P], qs, kr[:, w:w + P], start=False, stop=True).then_inc(S("scores_full"), 1)
                    x = 12 * (4 * t + q)
                    gate_matmuls(i, x, 6)
                    for g in range(2):
                        misc[g].wait(pe)
                        bank = take(2)
                        for kb in range(t + 1):
                            mm = nc.tensor.transpose(bank[:, kb * P:(kb + 1) * P], PB[q % 2][:, g, kb * P:(kb + 1) * P], IDENT[:])
                        mm.then_inc(S("probs_T_full"), 1)
                        gate_matmuls(i, x + 6 + 3 * g, 3)
                        misc[2].wait(pe)
                        for kb in range(t + 1):
                            mm = nc.tensor.matmul(out_bank[:, (4 * g + q) * HD:(4 * g + q + 1) * HD], PT[g][:, kb * P:(kb + 1) * P],
                                                  VT[:, ds(i, 1), kb, g * 64:g * 64 + 64][:, 0, :], start=kb == 0, stop=kb == t)
                        mm.then_inc(S("pv_done"), 1)
            for b in range(4):
                misc[b].leave(2)
        pe.wait_ge(S("oa_added"), 2 * TT + 1)
        for k in range(4):
            bank = take(k)
            for t in range(TT):
                mm = nc.tensor.transpose(bank[:, t * P:(t + 1) * P], OA[:, t, k * P:(k + 1) * P], IDENT[:])
            mm.then_inc(S("oa_T"), 1)
        s0, _, b0, _ = PH["branch2"]
        for k in range(4):
            misc[k].wait(pe)
        with pe.Fori(0, 2) as i:
            for j in range(2):
                pe.wait_ge(S("lo_done"), s0 + j + 1 + 2 * i)
                for b in range(4):
                    hi, lo = ((OAHI, OALO), (OBHI, OBLO))[b % 2]
                    m = b0 + 4 * j + b
                    gemm(G[m % 4], (evac[m % 4], m // 4 + 2 + 2 * i), j, range(4 * (b % 2), 4 * (b % 2) + 4),
                         P * (b // 2), h(hi), h(lo))
        run("wout", h(HHI), h(HLO), ready=h_ready(H2 + KT))
        mean_of_sum(M[0], 3 * (KT + 1))
        fbase = H2 + 3 * KT
        run("fup0", h(HHI), h(HLO), ready=h_ready(H2 + 2 * KT))
        run("fup1", h(HHI), h(HLO))
        run("fdown0", h(FHI[0]), h(FLO[0]), ready=h_ready(fbase))
        run("fup2", h(HHI), h(HLO))
        run("fdown1", h(FHI[1]), h(FLO[1]), ready=h_ready(fbase + KT))
        run("fdown2", h(FHI[0]), h(FLO[0]), kts=range(6), ready=h_ready(fbase + 2 * KT))
        mean_of_sum(M[0], 4 * (KT + 1))
        for k in range(KT):
            pe.wait_ge(S("hs_ready"), 4 * KT + k + 1)
            if k >= 4:
                pe.wait_ge(S("out_ready"), k - 3)
            bank = M[k % 4]
            for t in range(TT):
                mm = nc.tensor.transpose(bank[:, t * P:(t + 1) * P], HS[k % 2][:, t * P:(t + 1) * P], IDENT[:])
            mm.then_inc(S("out_T"), 1)

    @block.scalar
    def _(act):
        for dst, src in [(IDENT[:], a["c_ident"]), (ROWS_T[0:N_ROWS, :], a["rows"]),
                         (CROWS_T[0:CONV_K * CC, :], a["conv_w"][0].rearrange("k (c p) -> (k c) p", p=P)),
                         (RECIP[:], a["c_recip"].rearrange("p (g n) -> p g n", n=16)),
                         (ROT[:], a["c_rot"]), (CAUS32[:], a["c_causal"]),
                         (CMPM32[:], a["c_cmp_mask"].rearrange("p (t n) -> p t n", n=32)),
                         (W2G[0:16, :], a["gla_gate_w2_2"][0])]:
            act.dma_start(dst, src).then_inc(S("consts_loaded"), 16)
        act.dma_start(POOLW[:], a["pool_w"][0].rearrange("g c d -> c g d")).then_inc(S("pool_w_loaded"), 16)
        root = Count(S("root_ready"))

        def split_hi(s, par, i=0, kts=KT):
            act.wait_ge(raw_ready[par], 32 * (s // 2 + 1 + i) + (32 if s >= PH["nsa"][0] + 3 else 0))
            if s >= 2:
                per = BLOCKS_BEFORE[s] - BLOCKS_BEFORE[s - 1]
                act.wait_ge(S("block_full"), BLOCKS_BEFORE[s - 1] + 2 * per * i)
            nc.scalar.activation(WHI[par][:, 0:kts, :], RAW[par][:, 0:kts, :], ACT.Copy).then_inc(S("hi_done"), 1)

        def full(m, i=0, per=0):
            act.wait_ge(S("block_full"), m + 1 + i * per)

        def squares(used, x_base):
            for k in range(KT):
                act.wait_ge(S("x_ready"), x_base + k + 1)
                if k >= 2:
                    act.wait_ge(S("sq_used"), used + k - 1)
                nc.scalar.activation(SQ[k % 2][:], XT[:, k, :], ACT.Square).then_inc(S("sq_ready"), 1)

        def take_root(bank, sem, value):
            act.wait_ge(sem, value)
            root.inc(nc.scalar.activation(RS[:], bank[:], ACT.Sqrt, bias=EPSB[:]))

        def h_hi(base):
            for k in range(KT):
                act.wait_ge(S("hs_ready"), base + k + 1)
                nc.scalar.activation(HHI[:, k, :], HS[k % 2][:], ACT.Copy).then_inc(S("hhi_ready"), 1)

        def run(name, evacuate, lo_slab=0, slabs=None, next_kts=KT):
            s0, n, b0, bps = PH[name]
            n = slabs or n
            s0, b0 = s0 + lo_slab, b0 + lo_slab * bps
            with act.Fori(0, n // 2) as i:
                for j in range(2):
                    split_hi(s0 + j + 1, (s0 + j + 1) % 2, i)
                    for b in range(bps):
                        evacuate(bps * j + b, b0 + bps * j + b, i)

        for k in range(KT):
            act.wait_ge(S("x_transposed"), k + 1)
            nc.scalar.activation(XT[:, k, :], G[k % 4][:], ACT.Copy).then_inc(evac[k % 4], 1)
        act.wait_ge(S("eps_ready"), 1)
        for k in range(KT):
            act.wait_ge(evac[k % 4], k // 4 + 1)
            if k >= 2:
                act.wait_ge(S("sq_used"), k - 1)
            nc.scalar.activation(SQ[k % 2][:], XT[:, k, :], ACT.Square).then_inc(S("sq_ready"), 1)
        split_hi(0, 0)
        take_root(M[0], S("mean_ready"), 1)
        h_hi(0)

        def merge_gate(j, m, i):
            full(m, i, 4)
            nc.scalar.activation(GT[:, j + (m - j - 12) + 4 * i, :], G[m % 4][:], ACT.Tanh, scale=0.5).then_inc(evac[m % 4], 1)

        for c in range(CC):
            split_hi(c + 1, (c + 1) % 2)
            m = 2 * c + 1
            full(m)
            if c >= 2:
                act.wait_ge(*evac_at(m - 5))
            nc.scalar.activation(SG[c % 2][:], G[m % 4][:], ACT.Tanh, scale=0.5).then_inc(evac[m % 4], 1)
        for j in range(2):
            split_hi(CC + j + 1, (CC + j + 1) % 2)
            for b in range(2):
                g, m = 2 * j + b, 2 * (CC + j) + b
                full(m)
                if g:
                    act.wait_ge(S("pooled_ready"), g)
                else:
                    act.wait_ge(S("pads_ready"), 2)
                nc.scalar.activation(UP[:, 16:16 + T], G[m % 4][:], ACT.Copy).then_inc(evac[m % 4], 1)
        run("in", merge_gate, lo_slab=6, slabs=4)
        for g in range(POOL_G):
            act.wait_ge(S("mixed"), g + 1)
            nc.scalar.activation(PHI[:, g, :], M[g][:], ACT.Copy, scale=col("pool_scale", g)).then_inc(S("pool_hi_ready"), 1)

        def gates(s):
            split_hi(s + 1, (s + 1) % 2)
            for m in (2 * s, 2 * s + 1):
                full(m)
                nc.scalar.activation(GT[:, m - 12, :], G[m % 4][:], ACT.Tanh, scale=0.5).then_inc(evac[m % 4], 1)

        for s in (10, 11):
            gates(s)
        for c in range(CC):
            act.wait_ge(S("centred"), c + 1)
            nc.scalar.activation(PLD[:, c, :], CV[:, c, :], ACT.Square).then_inc(S("lsq_ready"), 1)
        for s in (12, 13):
            gates(s)
        take_root(M[1], S("ln_var"), 1)
        for c in range(CC):
            act.wait_ge(S("ln_ready"), c + 1)
            if c >= 2:
                act.wait_ge(S("silu_ready"), c - 1)
            nc.scalar.activation(SQ[c % 2][:], CV[:, c, :], ACT.Tanh, scale=0.5).then_inc(S("ln_tanh"), 1)
            if c >= 1:
                act.wait_ge(S("silu_ready"), c)
                nc.scalar.activation(CHI[:, c - 1, :], CV[:, c - 1, :], ACT.Copy, scale=0.5).then_inc(S("chi_ready"), 1)
        act.wait_ge(S("silu_ready"), CC)
        nc.scalar.activation(CHI[:, CC - 1, :], CV[:, CC - 1, :], ACT.Copy, scale=0.5).then_inc(S("chi_ready"), 1)
        def merged_hi(name, base, scale):
            s0, n, b0, bps = PH[name]
            with act.Fori(0, n // 2) as i:
                for j in range(2):
                    split_hi(s0 + j + 1, (s0 + j + 1) % 2, i)
                    for q in range(2):
                        k = 2 * j + q
                        act.wait_ge(S("merged_ready"), base + k + 1 + 4 * i)
                        nc.scalar.activation(HHI[:, k + 4 * i, :], HS[k % 2][:], ACT.Copy, scale=scale).then_inc(S("hhi_ready"), 1)

        merged_hi("branch", 0, 0.5)
        def copy_square(name):
            def evacuate(j, m, i):
                full(m, i, 4)
                nc.scalar.activation(Y[:, j + 4 * i, :], G[m % 4][:], ACT.Copy).then_inc(S("y_ready"), 1)
                act.wait_ge(S("sq_added"), j + 1 + 4 * i)
                nc.scalar.activation(SQ[j % 2][:], G[m % 4][:], ACT.Square).then_inc(evac[m % 4], 1)
            return evacuate

        run("wo", copy_square("wo"))
        take_root(M[0], S("mean_ready"), 2)
        squares(13, 0)
        take_root(M[0], S("mean_ready"), 3)
        h_hi(KT)
        def up_evac(ch):
            def evacuate(j, m, i):
                full(m, i, 4)
                r = ch * KT + j + 4 * i
                act.wait_ge(*evac_at(m - 2, i, 4))
                nc.scalar.activation(RL[j % 2][:], G[m % 4][:], ACT.Relu).then_inc(S("relu_ready"), 1)
                act.wait_ge(*evac_at(m, i, 4))
                nc.scalar.activation(FHI[ch % 2][:, j + 4 * i, :], FF[j % 2][:], ACT.Copy).then_inc(S("fhi_ready"), 1)
            return evacuate

        def nothing(j, m, i):
            pass

        def first_copy(j, m, i):
            full(m, i, 4)
            nc.scalar.activation(Y[:, j + 4 * i, :], G[m % 4][:], ACT.Copy).then_inc(evac[m % 4], 1)

        def last_square(base):
            def evacuate(j, m, i):
                act.wait_ge(*evac_at(m, i, 4))
                act.wait_ge(S("sq_added"), base + j + 1 + 4 * i)
                nc.scalar.activation(SQ[j % 2][:], Y[:, j + 4 * i, :], ACT.Square).then_inc(S("ysq_ready"), 1)
            return evacuate

        run("up0", up_evac(0))
        run("up1", up_evac(1))
        run("down0", first_copy)
        run("up2", up_evac(2))
        run("down1", nothing)
        run("up3", up_evac(3))
        run("down2", nothing)
        run("down3", last_square(KT + 1))
        take_root(M[0], S("mean_ready"), 4)
        squares(20, KT)
        take_root(M[0], S("mean_ready"), 5)
        h_hi(2 * KT)
        s0, _, m0, _ = PH["small"]
        A_, same = nc.scalar.activation, Count(S("scalar_step"))

        def split(j):
            split_hi(s0 + j, (s0 + j) % 2)

        def copy_out(m, dst, func=ACT.Copy, **kw):
            full(m)
            A_(dst, G[m % 4][:], func, **kw).then_inc(evac[m % 4], 1)

        split(1)
        copy_out(m0, SMALL[:])
        split(2)
        for j in range(2):
            copy_out(m0 + 1 + j, QG[:, j, :], scale=GLA_DK ** -0.5)
        act.wait_ge(S("gates_T"), 1)
        A_(GTH[:], M[1][:, 0:TT * 64].rearrange("p (t n) -> p t n", n=64)[:, :, 32:56], ACT.Tanh, scale=0.5).then_inc(read[1], 1)
        for j in range(2):
            act.wait_ge(read[2 + j], 1)
            same.inc(A_(SQ[j][:], QL[:, j, :], ACT.Abs))
        act.wait_ge(S("ones_ready"), 1)
        for j in range(2):
            same.wait(act, 1)
            same.inc(A_(SQ[j][:], SQ[j][:], ACT.Exp, scale=-1.0))
        for j in range(2):
            same.wait(act, 1 - j)
            A_(HS[j][:], SQ[j][:], ACT.Ln, bias=ONEB[:]).then_inc(S("softplus_ready"), 1)
        split(3)
        for j in range(2):
            copy_out(m0 + 3 + j, KG[:, j, :])
        split(4)
        for hd in range(2):
            copy_out(m0 + 5 + hd, VS[hd][:])
        split(5)

        def v_out(hd):
            act.wait_ge(S("v_T"), hd + 1)
            A_(VG[:, :, hd, :], M[hd][:].rearrange("p (c d) -> p c d", d=P), ACT.Copy).then_inc(read[hd], 1)

        for hd in range(2):
            v_out(hd)
        for hd in range(2):
            copy_out(m0 + 7 + hd, VS[hd][:])
        split(6)

        def r_out(hd):
            full(m0 + 9 + hd)
            A_(RG[:, hd, :], G[(m0 + 9 + hd) % 4][:], ACT.Tanh, scale=0.5).then_inc(S("r_tanh"), 1)

        r_out(0)
        r_out(1)
        v_out(2)
        v_out(3)
        split(7)
        r_out(2)
        r_out(3)

        def level(l):
            for j in range(2):
                act.wait_ge(S("dd_ready"), 2 * l + j + 1)
                same.inc(A_(HS[j][:], HS[j][:], ACT.Abs))
                same.wait(act)
                if l:
                    act.wait_ge(S("ql_ready"), 2 * l - 1 + j)
                    act.wait_ge(S("kl_ready"), 2 * l - 1 + j)
                A_(SQ[j][:], HS[j][:], ACT.Exp, scale=-1.0 / 16).then_inc(S("decay_ready"), 1)

        mk = BLOCKS_BEFORE[s0 + 7]
        dests = [RAWC[:, 0, :], RAWC[:, 1, :], KR[:, 0, :], VS[0][:], KR[:, 1, :], VS[1][:]] + [QR[:, q, :] for q in range(4)]
        level(0)
        for k in range(10):
            if k % 2 == 0:
                split(8 + k // 2)
            copy_out(mk + k, dests[k], scale=1.0 if k < 6 else HD ** -0.5)
            if k < LEVELS - 1:
                level(k + 1)
            for i in range(2):
                if k == 4 + 2 * i:
                    act.wait_ge(S("vb_T"), i + 1)
                    A_(VT[:, i, :, :], M[0][:].rearrange("p (c d) -> p c d", d=P), ACT.Copy).then_inc(read[0], 1)
        for j in range(2):
            act.wait_ge(S("ql_ready"), 2 * LEVELS - 1 + j)
            act.wait_ge(S("kl_ready"), 2 * LEVELS - 1 + j)
            A_(SQ[j][:], CUM[:, j, :], ACT.Exp, scale=1.0 / 16).then_inc(S("q_decay"), 1)
            A_(EL[:, j, :], CUM[:, j, P - 1:T:P], ACT.Exp, scale=1.0 / 16).then_inc(S("chunk_decay"), 1)
        for j in range(2):
            act.wait_ge(S("dd_ready"), 2 * LEVELS + j + 1)
            same.inc(A_(HS[j][:], HS[j][:], ACT.Abs))
            same.wait(act)
            act.wait_ge(S("ql_ready"), 2 * LEVELS + 1 + j)
            A_(SQ[j][:], HS[j][:], ACT.Exp, scale=-1.0 / 16).then_inc(S("decay_ready"), 1)
        for j in range(2):
            act.wait_ge(S("k_T"), j + 1)
            A_(KTOK[:, :, j * P:(j + 1) * P], M[j][:].rearrange("p (c d) -> p c d", d=P), ACT.Copy).then_inc(read[j], 1)
        act.wait_ge(S("gla_out_full"), 4)
        for hd in range(GLA_H):
            A_(OSB[:, hd, :], M[hd][:], ACT.Copy).then_inc(read[hd], 1)
        for hd in range(GLA_H):
            act.wait_ge(read[hd], (13, 12, 12, 12)[hd])
            if hd >= 2:
                act.wait_ge(S("gla_mean"), hd - 1)
            A_(SQ[hd % 2][:], OSB[:, hd, :], ACT.Square).then_inc(S("gla_sq_ready"), 1)
        for hd in range(GLA_H):
            act.wait_ge(S("gla_mean"), hd + 1)
            A_(RS4[:, hd, :], M[hd][:], ACT.Sqrt, bias=EPSB[:]).then_inc(read[hd], 1)
        for hd in range(GLA_H):
            act.wait_ge(S("ob_ready"), hd + 1)
            A_(OBHI[:, hd, :], OSB[:, hd, :], ACT.Copy, scale=0.5).then_inc(S("ob_hi_ready"), 1)
        act.wait_ge(S("ob_lo_ready"), 4)
        for n in range(4):
            kv, g = n // 2, n % 2
            A_(Z[64:128, n, 0:T - 1], RAWC[64 * g:64 * g + 64, kv, 1:T], ACT.Copy).then_inc(S("windows_b"), 1)
        for kv in range(2):
            act.wait_ge(read[2 + kv], 15)
            A_(HT[kv][:], HX[kv][:], ACT.Tanh, scale=0.5).then_inc(S("hidden_tanh"), 1)
        for g in range(2):
            act.wait_ge(read[2 + g], 16)
            x = PC[:, :, 4 * g:4 * g + 4, :]
            A_(x, x, ACT.Exp).then_inc(S("cmp_probs"), 1)
        for p in range(2):
            act.wait_ge(S("probs_T_full"), 2 * (p + 1))
            A_(PCT[:, 4 * p:4 * p + 4, :], M[p][:].rearrange("p (c d) -> p c d", d=P), ACT.Copy).then_inc(read[p], 1)
        sM, _, mM, _ = PH["merge"]
        act.wait_ge(S("ropes_ready"), 2)
        act.wait_ge(S("windows_a"), 4)
        A_(KNOW[:], KR[:, 0, :], ACT.Copy).then_inc(S("keys_moved"), 1)
        with act.Fori(0, 2) as i:
            for t in range(TT):
                for q in range(4):
                    step = 4 * t + q
                    if q == 0:
                        split_hi(sM + t + 1, (sM + t + 1) % 2, 2 * i)
                    act.wait_ge(S("neg_ready"), step + 1 + 16 * i)
                    for g in range(2):
                        w = (t + 1) * P
                        act.wait_ge(S("probs_T_full"), 2 * step + 1 + g + 32 * i)
                        A_(PB[q % 2][:, g, 0:w], M[g][:, 0:w], ACT.Exp, bias=NG[q % 2][:, g:g + 1],
                           accum_out=SUM[t % 2][:, 4 * g + q:4 * g + q + 1]).then_inc(read[g], 1)
                    if step == 15:
                        act.wait_ge(S("keys_moved"), 1 + i)
                        A_(KNOW[:], KR[:, 1, :], ACT.Copy).then_inc(S("keys_moved"), 1)
                    if q % 2:
                        m = mM + 2 * t + q // 2
                        full(m, i, 8)
                        A_(GT[:, 2 * t + q // 2 + 8 * i, :], G[m % 4][:], ACT.Tanh, scale=0.5).then_inc(evac[m % 4], 1)
        for k in range(4):
            act.wait_ge(S("oa_T"), k + 1)
            A_(OAHI[:, k, :], M[k][:], ACT.Copy).then_inc(S("oa_hi_ready"), 1)
        merged_hi("branch2", KT, 0.5)

        def x_square(base):
            def evacuate(j, m, i):
                act.wait_ge(*evac_at(m, i, 4))
                act.wait_ge(S("sq_added"), base + j + 1 + 4 * i)
                A_(SQ[j % 2][:], XT[:, j + 4 * i, :], ACT.Square).then_inc(S("ysq_ready"), 1)
            return evacuate

        run("wout", x_square(2 * (KT + 1)))
        take_root(M[0], S("mean_ready"), 6)
        h_hi(3 * KT)
        def gate_up(name, ch):
            s0, n, b0, _ = PH[name]
            with act.Fori(0, n // 2) as i:
                for j in range(2):
                    split_hi(s0 + j + 1, (s0 + j + 1) % 2, i)
                    for b in range(2):
                        m = b0 + 2 * j + b
                        if j == 0:
                            full(m, i, 4)
                            A_(SQ[b][:], G[m % 4][:], ACT.Tanh, scale=0.5).then_inc(S("ffn_tanh"), 1)
                        else:
                            act.wait_ge(*evac_at(m, i, 4))
                            A_(FHI[ch % 2][:, b + 2 * i, :], FG[b][:], ACT.Copy, scale=0.5).then_inc(S("fhi_ready"), 1)

        gate_up("fup0", 0)
        gate_up("fup1", 1)
        run("fdown0", nothing)
        gate_up("fup2", 2)
        run("fdown1", nothing)
        s0, _, b0, _ = PH["fdown2"]
        last = x_square(3 * (KT + 1))
        for j in range(4):
            if j < 3:
                split_hi(s0 + j + 1, (s0 + j + 1) % 2)
            for b in range(2):
                last(2 * j + b, b0 + 2 * j + b, 0)
        take_root(M[0], S("mean_ready"), 7)
        for k in range(KT):
            act.wait_ge(S("out_T"), k + 1)
            A_(OTK[:, :, k * P:(k + 1) * P], M[k % 4][:].rearrange("p (t d) -> p t d", d=P), ACT.Copy).then_inc(S("out_ready"), 1)

    @block.vector
    def _(dve):
        V = nc.vector
        V.memset(EPSB[:], EPS).then_inc(S("eps_ready"), 1)
        for n in (128, 512):
            V.memset(INV[n][:], 1.0 / n)
        V.memset(INV[1024][:], 1.0 / 1024).then_inc(S("inv_ready"), 1)
        rstd = Count(S("rstd_ready"))
        step = Count(S("vector_step"))

        def split_lo(s, par, i=0, kts=KT):
            dve.wait_ge(S("hi_done"), s + 1 + 2 * i)
            V.tensor_tensor(WLO[par][:, 0:kts, :], RAW[par][:, 0:kts, :], f(WHI[par][:, 0:kts, :]), SUB).then_inc(S("lo_done"), 1)

        def full(m, i=0, per=0):
            dve.wait_ge(S("block_full"), m + 1 + i * per)

        def invert(root_at, used=None):
            dve.wait_ge(S("root_ready"), root_at)
            if used:
                dve.wait_ge(*used)
            rstd.inc(V.reciprocal(RSTD[:], RS[:]))
            rstd.wait(dve)

        def h_lo(base, gain, hi_base=None):
            hi_base = base if hi_base is None else hi_base
            """h = x gain / rms in two float32r parts; the product of a tile runs ahead of the split before it."""
            for k in range(KT + 1):
                if k < KT:
                    if k >= 2:
                        dve.wait_ge(S("hlo_ready"), base + k - 1)
                    V.scalar_tensor_tensor(HS[k % 2][:], XT[:, k, :], col(gain, k), RSTD[:], MUL, MUL).then_inc(S("hs_ready"), 1)
                if k:
                    dve.wait_ge(S("hhi_ready"), hi_base + k)
                    V.tensor_tensor(HLO[:, k - 1, :], HS[(k - 1) % 2][:], f(HHI[:, k - 1, :]), SUB).then_inc(S("hlo_ready"), 1)

        def residual(gain, y_sem, y_at):
            for k in range(KT):
                V.scalar_tensor_tensor(Y[:, k, :], Y[:, k, :], col(gain, k), RSTD[:], MUL, MUL).then_inc(S("y_scaled"), 1)
                if k:
                    dve.wait_ge(S("y_scaled"), scaled[0] + k)
                    V.tensor_tensor(XT[:, k - 1, :], XT[:, k - 1, :], Y[:, k - 1, :], ADD).then_inc(S("x_ready"), 1)
            dve.wait_ge(S("y_scaled"), scaled[0] + KT)
            V.tensor_tensor(XT[:, KT - 1, :], XT[:, KT - 1, :], Y[:, KT - 1, :], ADD).then_inc(S("x_ready"), 1)
            scaled[0] += KT

        scaled = [0]

        def run(name, evacuate, lo_slab=0, slabs=None):
            s0, n, b0, bps = PH[name]
            n = slabs or n
            s0, b0 = s0 + lo_slab, b0 + lo_slab * bps
            with dve.Fori(0, n // 2) as i:
                for j in range(2):
                    split_lo(s0 + j + 1, (s0 + j + 1) % 2, i)
                    for b in range(bps):
                        evacuate(bps * j + b, b0 + bps * j + b, i)

        dve.wait_ge(S("consts_loaded"), CONST_DMAS * 16)
        V.tensor_copy(IDENTB[:], IDENT[:])
        V.tensor_copy(CAUSB[:], CAUS32[:])
        V.tensor_copy(CMPMB[:], CMPM32[:]).then_inc(S("masks_ready"), 1)
        dve.wait_ge(S("rows_transposed"), 2)
        V.tensor_copy(PV[:, 0:N_ROWS], M[1][:, 0:N_ROWS]).then_inc(S("cols_ready"), 1)
        V.tensor_scalar(CW[:, 0:CONV_K * CC], M[2][:, 0:CONV_K * CC], 0.5, None, MUL).then_inc(S("cols_ready"), 1)
        dve.wait_ge(S("cols_ready"), 2)
        split_lo(0, 0)
        invert(1)
        h_lo(0, "norm_mix_pre")

        def conv(c, taps, i=0):
            for k in taps:
                x, w = VP[:, c, k:k + T], CW[:, ds(k * CC + c, 1)]
                y = CV[:, c, :]
                if k == 0:
                    step.inc(V.tensor_scalar(y, x, w, PV[:, ds(ROW0["conv_b"] + c, 1)], MUL, ADD))
                elif k < CONV_K - 1:
                    step.wait(dve)
                    step.inc(V.scalar_tensor_tensor(y, x, w, y, MUL, ADD))
                else:
                    step.wait(dve)
                    V.scalar_tensor_tensor(y, x, w, y, MUL, ADD).then_inc(S("conv_ready"), 1)

        def glu(c):
            m = 2 * c
            dve.wait_ge(*evac_at(m + 1))
            V.scalar_tensor_tensor(VP[:, c, 30:30 + T], SG[c % 2][:], 1.0, G[m % 4][:], ADD, MUL).then_inc(evac[m % 4], 1)

        half = (range(0, 16), range(16, CONV_K))
        dve.wait_ge(S("pads_ready"), 2)
        for c in range(CC):
            split_lo(c + 1, (c + 1) % 2)
            glu(c)
            if c >= 2:
                dve.wait_ge(*evac_at(0))
                conv(0, half[c - 2])
        for j in range(2):
            split_lo(CC + 1 + j, (CC + 1 + j) % 2)
            dve.wait_ge(*evac_at(2))
            conv(1, half[j])
            for g in (2 * j, 2 * j + 1):
                dve.wait_ge(S("window_summed"), g + 1)
                total = S2[g % 2]
                w = 2 << g
                V.scalar_tensor_tensor(PLD[:, g, 16:T], total[:, 32:16 + T], 1.0 / w, UP[:, 32:16 + T], MUL, SUB)
                if g:
                    dve.wait_ge(S("pooled_ready"), g)
                step.inc(V.tensor_tensor(TMP16[:], total[:, 16:32], RECIP[:, g, :], MUL))
                step.wait(dve)
                V.tensor_tensor(PLD[:, g, 0:16], TMP16[:], UP[:, 16:32], SUB).then_inc(S("pooled_ready"), 1)
        with dve.Fori(0, 2) as i:
            step.enter(i, CONV_K - 1)
            for j in range(2):
                split_lo(7 + j, (7 + j) % 2, i)
                dve.wait_ge(*evac_at(6))
                conv(2 + i, half[j])
            step.leave(2)
        for g in range(POOL_G):
            dve.wait_ge(S("pool_hi_ready"), g + 1)
            V.scalar_tensor_tensor(PLO[:, g, :], M[g][:], col("pool_scale", g), f(PHI[:, g, :]), MUL, SUB).then_inc(S("pool_lo_ready"), 1)
        split_lo(11, 1)
        dve.wait_ge(S("ln_mean"), 1)
        dve.wait_ge(S("conv_ready"), CC)
        for c in range(CC):
            V.tensor_tensor(CV[:, c, :], CV[:, c, :], M[0][:], SUB).then_inc(S("centred"), 1)
        split_lo(12, 0)
        split_lo(13, 1)
        split_lo(14, 0)
        invert(2, (S("hs_ready"), KT))
        dve.wait_ge(S("centred"), CC)
        dve.wait_ge(S("lsq_ready"), CC)
        for c in range(CC):
            step.inc(V.tensor_tensor(CV[:, c, :], CV[:, c, :], RSTD[:], MUL))
        for c in range(CC):
            step.wait(dve, CC - 1 - c)
            V.tensor_scalar(CV[:, c, :], CV[:, c, :], col("conv_ln_g", c), col("conv_ln_b", c), MUL, ADD).then_inc(S("ln_ready"), 1)
        for c in range(CC):
            dve.wait_ge(S("ln_tanh"), c + 1)
            V.scalar_tensor_tensor(CV[:, c, :], SQ[c % 2][:], 1.0, CV[:, c, :], ADD, MUL).then_inc(S("silu_ready"), 1)
            if c:
                dve.wait_ge(S("chi_ready"), c)
                V.scalar_tensor_tensor(CLO[:, c - 1, :], CV[:, c - 1, :], 0.5, f(CHI[:, c - 1, :]), MUL, SUB).then_inc(S("clo_ready"), 1)
        dve.wait_ge(S("chi_ready"), CC)
        V.scalar_tensor_tensor(CLO[:, CC - 1, :], CV[:, CC - 1, :], 0.5, f(CHI[:, CC - 1, :]), MUL, SUB).then_inc(S("clo_ready"), 1)
        def merge(name, hi_base, scale):
            s0, n, b0, bps = PH[name]
            with dve.Fori(0, n // 2) as i:
                for j in range(2):
                    split_lo(s0 + j + 1, (s0 + j + 1) % 2, i)
                    for q in range(2):
                        k = 2 * j + q
                        for side in range(2):
                            m = b0 + 4 * j + 2 * q + side
                            full(m, i, 8)
                            gt = GT[:, k + 4 * i + KT * side, :]
                            V.scalar_tensor_tensor(gt, gt, 1.0, G[m % 4][:], ADD, MUL).then_inc(evac[m % 4], 1)
                    for q in range(2):
                        k = 2 * j + q
                        dve.wait_ge(S("hhi_ready"), hi_base + k + 1 + 4 * i)
                        V.scalar_tensor_tensor(HLO[:, k + 4 * i, :], HS[k % 2][:], scale, f(HHI[:, k + 4 * i, :]), MUL, SUB).then_inc(S("hlo_ready"), 1)

        merge("branch", KT, 0.5)
        def nothing(j, m, i):
            pass

        run("wo", nothing)
        invert(3, (S("silu_ready"), CC))
        dve.wait_ge(S("y_ready"), KT)
        residual("norm_mix_post", "y_ready", KT)
        invert(4, (S("y_scaled"), KT))
        h_lo(2 * KT, "norm_mlp_pre")
        def up_evac(ch):
            def evacuate(j, m, i):
                r = ch * KT + j + 4 * i
                dve.wait_ge(S("relu_ready"), r + 1)
                dve.wait_ge(S("hlo_ready"), 3 * KT + r)
                V.tensor_tensor(FF[j % 2][:], RL[j % 2][:], G[m % 4][:], MUL).then_inc(evac[m % 4], 1)
                dve.wait_ge(S("fhi_ready"), r + 1)
                V.tensor_tensor(FLO[ch % 2][:, j + 4 * i, :], FF[j % 2][:], f(FHI[ch % 2][:, j + 4 * i, :]), SUB).then_inc(S("hlo_ready"), 1)
            return evacuate

        def add_block(j, m, i):
            full(m, i, 4)
            y = Y[:, j + 4 * i, :]
            V.tensor_tensor(y, y, G[m % 4][:], ADD).then_inc(evac[m % 4], 1)

        run("up0", up_evac(0))
        run("up1", up_evac(1))
        run("down0", nothing)
        run("up2", up_evac(2))
        run("down1", add_block)
        run("up3", up_evac(3))
        run("down2", add_block)
        run("down3", add_block)
        invert(5, (S("hs_ready"), 2 * KT))
        dve.wait_ge(S("ysq_ready"), KT)
        residual("norm_mlp_post", None, None)
        invert(6, (S("y_scaled"), 2 * KT))
        h_lo(7 * KT, "norm_mix_2", 3 * KT)
        s0, _, m0, _ = PH["small"]

        def split(j):
            split_lo(s0 + j, (s0 + j) % 2)

        def chunks(ap, n=P):
            return ap.rearrange("p (c n) -> p c n", n=n)

        split(1)
        split(2)
        dve.wait_ge(read[1], 1)
        V.tensor_scalar(GATES[:], GTH[:], 0.5, 0.5, MUL, ADD).then_inc(S("gates_ready"), 1)
        dve.wait_ge(S("masks_small"), 1)
        for j in range(2):
            dve.wait_ge(S("decay_in"), j + 1)
            V.tensor_scalar(QL[:, j, :], M[2 + j][:], col("gla_gate_b_2", j), None, ADD).then_inc(read[2 + j], 1)
        dve.wait_ge(S("gla_consts"), 32)
        for j in range(2):
            dve.wait_ge(S("softplus_ready"), j + 1)
            step.inc(V.scalar_tensor_tensor(QL[:, j, :], QL[:, j, :], 0.0, HS[j][:], ALU.min, SUB))
            step.wait(dve)
            V.tensor_tensor_scan(CUM[:, j, :], RESET[:], QL[:, j, :], 0.0, MUL, ADD).then_inc(S("cum_ready"), 1)
        for j in range(3, 7):
            split(j)

        def r_gate(hd):
            m = m0 + 9 + hd
            dve.wait_ge(S("r_tanh"), hd + 1)
            V.scalar_tensor_tensor(RG[:, hd, :], RG[:, hd, :], 1.0, G[m % 4][:], ADD, MUL).then_inc(evac[m % 4], 1)

        r_gate(0)
        r_gate(1)
        split(7)
        r_gate(2)
        r_gate(3)

        def distance(l):
            n = P >> l if l < LEVELS else P
            at_ = n // 2 - 1 if l < LEVELS else P - 1
            for j in range(2):
                dve.wait_ge(S("cum_ready"), 2)
                if l:
                    dve.wait_ge(S("decay_ready"), 2 * l - 1 + j)
                c = chunks(CUM[:, j, :], n)
                V.tensor_tensor(chunks(HS[j][:], n), c, c[:, :, at_:at_ + 1].broadcast_to([P, T // n, n]), SUB).then_inc(S("dd_ready"), 1)

        def decayed_q(l):
            for j in range(2):
                dve.wait_ge(S("decay_ready"), 2 * l + j + 1)
                if l:
                    dve.wait_ge(S("level_full"), 4 * l)
                V.tensor_tensor(QL[:, j, :], QG[:, j, :], SQ[j][:], MUL).then_inc(S("ql_ready"), 1)

        def pick(l):
            for hd in range(GLA_H):
                dve.wait_ge(S("level_full"), 4 * l + hd + 1)
                V.copy_predicated(chunks(A[:, hd, :]), LEVM[:, l:l + 1, :].broadcast_to([P, TT, P]), chunks(M[hd][:])).then_inc(read[hd], 1)

        dve.wait_ge(S("attn_zero"), 1)
        distance(0)
        for k in range(10):
            if k % 2 == 0:
                split(8 + k // 2)
            if k < LEVELS:
                decayed_q(k)
                if k + 1 < LEVELS:
                    distance(k + 1)
            if k <= LEVELS:
                pick(k)
        for j in range(2):
            dve.wait_ge(S("q_decay"), j + 1)
            V.tensor_tensor(QL[:, j, :], QG[:, j, :], SQ[j][:], MUL).then_inc(S("ql_ready"), 1)
        distance(LEVELS)
        dve.wait_ge(S("chunk_decay"), 2)
        for j in range(2):
            dve.wait_ge(S("update_full"), j + 1)
            u = M[2 + j]
            step.inc(V.tensor_copy(ST[:, j, 0, :], u[:, 0:P]))
            step.wait(dve)
            step.inc(V.scalar_tensor_tensor(ST[:, j, 1, :], ST[:, j, 0, :], EL[:, j, 1:2], u[:, P:2 * P], MUL, ADD))
            step.wait(dve)
            V.scalar_tensor_tensor(ST[:, j, 2, :], ST[:, j, 1, :], EL[:, j, 2:3], u[:, 2 * P:3 * P], MUL, ADD).then_inc(read[2 + j], 1)
        for hd in range(GLA_H):
            dve.wait_ge(read[hd], (14, 13, 13, 13)[hd])
            step.inc(V.reciprocal(RS4[:, hd, :], RS4[:, hd, :]))
            step.wait(dve)
            step.inc(V.scalar_tensor_tensor(OSB[:, hd, :], OSB[:, hd, :], col("gla_norm_2"), RS4[:, hd, :], MUL, MUL))
            step.wait(dve)
            V.tensor_tensor(OSB[:, hd, :], OSB[:, hd, :], RG[:, hd, :], MUL).then_inc(S("ob_ready"), 1)
        for hd in range(GLA_H):
            dve.wait_ge(S("ob_hi_ready"), hd + 1)
            V.scalar_tensor_tensor(OBLO[:, hd, :], OSB[:, hd, :], 0.5, f(OBHI[:, hd, :]), MUL, SUB).then_inc(S("ob_lo_ready"), 1)
        dve.wait_ge(S("rope_loaded"), 32)
        for n in range(6):
            dst = KR[:, n, :] if n < 2 else QT[:, n - 2, :]
            dve.wait_ge(S("rotated"), n + 1)
            if n >= 2:
                dve.wait_ge(S("ropes_ready"), n - 1)
            V.tensor_tensor(SQ[n % 2][:], M[n % 4][:], SIN[:], MUL).then_inc(read[n % 4], 1)
            dve.wait_ge(S("cos_ready"), n + 1)
            dve.wait_ge(read[n % 4], (15, 14, 14, 14, 16, 15)[n])
            V.tensor_tensor(dst, SQ[n % 2][:], HS[n % 2][:], ADD).then_inc(S("ropes_ready"), 1)
        for n in range(4):
            kv, g = n // 2, n % 2
            V.tensor_copy(Z[0:64, n, :], RAWC[64 * g:64 * g + 64, kv, :]).then_inc(S("windows_a"), 1)
        for kv in range(2):
            step.inc(V.memset(HX[kv][:], 0.0))
        for kv in range(2):
            u = M[2 + kv]
            dve.wait_ge(S("hidden_full"), kv + 1)
            step.inc(V.tensor_copy(HB[:, kv:kv + 1], u[:, 64:65]))
            step.wait(dve)
            V.tensor_scalar(chunks(HX[kv][:], 32)[:, :, 0:N_CMP], chunks(u[:, 0:64], 32)[:, :, 0:N_CMP],
                            HB[:, kv:kv + 1], None, ADD).then_inc(read[2 + kv], 1)
        for kv in range(2):
            dve.wait_ge(S("hidden_tanh"), kv + 1)
            V.scalar_tensor_tensor(HX[kv][:], HT[kv][:], 1.0, HX[kv][:], ADD, MUL).then_inc(S("hidden_ready"), 1)
        dve.wait_ge(S("kc_full"), 1)
        V.tensor_scalar(KC[:, 0:N_CMP], M[0][:, 0:N_CMP], 0.5, None, MUL).then_inc(read[0], 1)
        dve.wait_ge(S("vc_full"), 1)
        dve.wait_ge(S("blocks_zero"), 1)
        for g in range(2):
            for q in range(4):
                ins = V.tensor_scalar(VBD[32 * q:32 * q + 32, g, HD * q:HD * q + HD], M[1][0:32, HD * g:HD * g + HD], 0.5, None, MUL)
        ins.then_inc(read[1], 1)
        for g in range(2):
            x = M[2 + g][:].rearrange("p (t h n) -> p t h n", h=4, n=32)
            mx = MXC[:, 16 * g:16 * g + 16].rearrange("p (t h) -> p t h", h=4)
            dve.wait_ge(S("cmp_scores"), g + 1)
            step.inc(V.reduce_max(mx, x, AX.X))
            step.wait(dve)
            step.inc(V.tensor_scalar(mx, mx, -1e29, None, MAX))
            step.wait(dve)
            V.tensor_tensor(PC[:, :, 4 * g:4 * g + 4, :], x, mx.unsqueeze(3).broadcast_to([P, TT, 4, 32]), SUB).then_inc(read[2 + g], 1)
        for g in range(2):
            sm = SMC[:, 16 * g:16 * g + 16].rearrange("p (t h) -> p t h", h=4)
            dve.wait_ge(S("cmp_probs"), g + 1)
            step.inc(V.reduce_sum(sm, PC[:, :, 4 * g:4 * g + 4, :], AX.X))
            step.wait(dve)
            step.inc(V.tensor_scalar(sm, sm, 1e-30, None, MAX))
            step.wait(dve)
            step.inc(V.reciprocal(sm, sm))
            step.wait(dve)
            step.inc(V.tensor_tensor(FC[:].rearrange("p (t h) -> p t h", h=HEADS)[:, :, 4 * g:4 * g + 4], sm,
                                     GATES[:, :, 12 * g:12 * g + 12:3], MUL))
        step.wait(dve)
        for t in range(TT):
            dve.wait_ge(S("cmp_out_full"), t + 1)
            b = (2 + t) % 4
            V.tensor_tensor(chunks(OA[:, t, :], HD), chunks(M[b][:], HD),
                            FC[:, 8 * t:8 * t + 8].unsqueeze(2).broadcast_to([P, HEADS, HD]), MUL).then_inc(read[b], 1)
        sM = PH["merge"][0]
        with dve.Fori(0, 2) as i:
            step.enter(i, 2 * 16 + 2 * TT)
            for t in range(TT):
                w = (t + 1) * P
                for q in range(4):
                    st = 4 * t + q
                    if q == 0:
                        split_lo(sM + t + 1, (sM + t + 1) % 2, 2 * i)
                    for g in range(2):
                        dve.wait_ge(S("scores_full"), 2 * st + g + 1 + 32 * i)
                        step.inc(V.reduce_max(NM[q % 2][:, g:g + 1], M[g][:, 0:w], AX.X))
                    step.wait(dve)
                    V.tensor_scalar(NG[q % 2][:], NM[q % 2][:], -1.0, None, MUL).then_inc(S("neg_ready"), 1)
                    for g in range(2):
                        dve.wait_ge(S("probs_T_full"), 4 + 2 * st + g + 1 + 32 * i)
                        V.tensor_copy(PT[g][:, 0:w], M[2][:, 0:w]).then_inc(read[2], 1)
                dve.wait_ge(S("pv_done"), 8 * (t + 1) + 32 * i)
                step.inc(V.reciprocal(FS[:], SUM[t % 2][:]))
                step.wait(dve)
                step.inc(V.tensor_tensor(FS[:], FS[:], GATES[:, t, ds(1 + i, HEADS, step=3)], MUL))
                step.wait(dve)
                dve.wait_ge(S("oa_added"), t + 1 + 4 * i)
                V.tensor_tensor(chunks(OTMP[:], HD), chunks(M[3][:], HD),
                                FS[:].unsqueeze(2).broadcast_to([P, HEADS, HD]), MUL).then_inc(read[3], 1)
            step.leave(2)
        for k in range(4):
            dve.wait_ge(S("oa_hi_ready"), k + 1)
            V.tensor_tensor(OALO[:, k, :], M[k][:], f(OAHI[:, k, :]), SUB).then_inc(read[k], 1)
        merge("branch2", 4 * KT, 0.5)

        def add_to_x(j, m, i):
            full(m, i, 4)
            x = XT[:, j + 4 * i, :]
            V.tensor_tensor(x, x, G[m % 4][:], ADD).then_inc(evac[m % 4], 1)

        run("wout", add_to_x)
        invert(7, (S("hs_ready"), 3 * KT))
        h_lo(H2 + 2 * KT, "norm_ffn_2", 5 * KT)
        fbase = H2 + 3 * KT

        def gate_up(name, ch):
            s0, n, b0, _ = PH[name]
            with dve.Fori(0, n // 2) as i:
                for j in range(2):
                    split_lo(s0 + j + 1, (s0 + j + 1) % 2, i)
                    for b in range(2):
                        m = b0 + 2 * j + b
                        if j == 0:
                            dve.wait_ge(S("ffn_tanh"), KT * ch + b + 1 + 2 * i)
                            dve.wait_ge(*evac_at(m - 2, i, 4))
                            V.scalar_tensor_tensor(HS[b][:], SQ[b][:], 1.0, G[m % 4][:], ADD, MUL).then_inc(evac[m % 4], 1)
                        else:
                            k = KT * ch + b
                            full(m, i, 4)
                            dve.wait_ge(*evac_at(m - 2, i, 4))
                            dve.wait_ge(S("hlo_ready"), fbase + k - 1 + 2 * i)
                            V.tensor_tensor(FG[b][:], HS[b][:], G[m % 4][:], MUL).then_inc(evac[m % 4], 1)
                            dve.wait_ge(S("fhi_ready"), F2 + k + 1 + 2 * i)
                            V.scalar_tensor_tensor(FLO[ch % 2][:, b + 2 * i, :], FG[b][:], 0.5,
                                                   f(FHI[ch % 2][:, b + 2 * i, :]), MUL, SUB).then_inc(S("hlo_ready"), 1)

        gate_up("fup0", 0)
        gate_up("fup1", 1)
        run("fdown0", add_to_x)
        gate_up("fup2", 2)
        run("fdown1", add_to_x)
        s0, _, b0, _ = PH["fdown2"]
        for j in range(4):
            if j < 3:
                split_lo(s0 + j + 1, (s0 + j + 1) % 2)
            for b in range(2):
                add_to_x(2 * j + b, b0 + 2 * j + b, 0)
        invert(8, (S("hs_ready"), 4 * KT))
        for k in range(KT):
            if k >= 2:
                dve.wait_ge(S("out_T"), k - 1)
            V.scalar_tensor_tensor(HS[k % 2][:], XT[:, k, :], col("norm_final_2", k), RSTD[:], MUL, MUL).then_inc(S("hs_ready"), 1)

    @block.gpsimd
    def _(pool):
        Q = nc.gpsimd
        Q.memset(VP[:, :, 0:30], 0.0).then_inc(S("pads_ready"), 1)
        Q.memset(UP[:, 0:16], 0.0).then_inc(S("pads_ready"), 1)
        gstep = Count(S("gpsimd_step"))
        for g in range(POOL_G):
            m = 2 * CC + g
            pool.wait_ge(*evac_at(m))
            src = UP
            for l in range(g + 1):
                sh, lo = 1 << l, (2 << l) - 1
                dst = S2[l % 2]
                if l:
                    gstep.wait(pool)
                elif g:
                    pool.wait_ge(S("pooled_ready"), g)
                ins = Q.tensor_tensor(dst[:, lo:16 + T], src[:, lo:16 + T], src[:, lo - sh:16 + T - sh], ADD)
                if l < g:
                    gstep.inc(ins)
                else:
                    ins.then_inc(S("window_summed"), 1)
                src = dst
        def merge_sum(name, base, lo_base):
            s0, n, b0, bps = PH[name]
            with pool.Fori(0, n // 2) as i:
                for k in range(4):
                    m = b0 + 2 * k + 1
                    pool.wait_ge(*evac_at(m, i, 8))
                    pool.wait_ge(*evac_at(m - 1, i, 8))
                    pool.wait_ge(S("hlo_ready"), lo_base + k - 1 + 4 * i)
                    Q.tensor_tensor(HS[k % 2][:], GT[:, k + 4 * i, :], GT[:, KT + k + 4 * i, :], ADD).then_inc(S("merged_ready"), 1)

        merge_sum("branch", 0, KT)
        def add_squares(n, mean_at, ready):
            pool.wait_ge(S("mean_ready"), mean_at)
            Q.memset(SQA[:], 0.0).then_inc(S("sq_added"), 1)
            with pool.Fori(0, KT // 4) as i:
                for j in range(4):
                    pool.wait_ge(*ready(j, i))
                    pool.wait_ge(S("sq_added"), (KT + 1) * n + 1 + j + 4 * i)
                    Q.tensor_tensor(SQA[:], SQA[:], SQ[j % 2][:], ADD).then_inc(S("sq_added"), 1)

        b0 = PH["wo"][2]
        add_squares(0, 1, lambda j, i: evac_at(b0 + j, i, 4))
        add_squares(1, 3, lambda j, i: (S("ysq_ready"), j + 1 + 4 * i))
        pool.wait_ge(S("block_full"), PH["small"][2])
        for i, n in enumerate(("cmp_k_w1_2", "cmp_v_w1_2")):
            pool.dma_start(W1[i][:], a[n][0].rearrange("(j p) h -> p j h", p=P)).then_inc(S("cmp_loaded"), 16)
        pool.dma_start(LEV32[:], a["c_level"].rearrange("p (l t) -> p l t", t=P)).then_inc(S("gla_consts"), 16)
        pool.dma_start(RESET[:], a["c_reset"]).then_inc(S("gla_consts"), 16)
        pool.dma_start(SIN[:], a["c_sin"]).then_inc(S("rope_loaded"), 16)
        pool.wait_ge(S("gla_consts"), 32)
        Q.tensor_copy(LEVM[:], LEV32[:]).then_inc(S("masks_small"), 1)
        Q.memset(ONEB[:], 1.0).then_inc(S("ones_ready"), 1)
        Q.memset(A[:], 0.0).then_inc(S("attn_zero"), 1)
        pool.wait_ge(S("mean_ready"), 5)
        pool.dma_start(COS[:], a["c_cos"]).then_inc(S("rope_loaded"), 16)

        def decayed_k(l, at_):
            for j in range(2):
                pool.wait_ge(S("decay_ready"), at_ + j + 1)
                if l:
                    pool.wait_ge(S("level_full"), 4 * l)
                Q.tensor_tensor(KL[:, j, :], KG[:, j, :], SQ[j][:], MUL).then_inc(S("kl_ready"), 1)

        for l in range(LEVELS + 1):
            decayed_k(l, 2 * l)
        pool.wait_ge(S("gla_out_full"), GLA_H)
        for i, n in enumerate(("cmp_k_w2_2", "cmp_v_w2_2")):
            pool.dma_start(W2[i][:], a[n][0]).then_inc(S("cmp_loaded"), 16)
        pool.wait_ge(S("rope_loaded"), 32)
        for n in range(6):
            x = KR[:, n, :] if n < 2 else QR[:, n - 2, :]
            pool.wait_ge(S("rotated"), n + 1)
            if n >= 2:
                pool.wait_ge(S("ropes_ready"), n - 1)
            Q.tensor_tensor(HS[n % 2][:], x, COS[:], MUL).then_inc(S("cos_ready"), 1)
        pool.wait_ge(S("windows_a"), 4)
        pool.wait_ge(S("windows_b"), 4)
        Q.memset(VBD[:], 0.0).then_inc(S("blocks_zero"), 1)
        Q.memset(OTMP[:], 0.0).then_inc(S("oa_added"), 1)
        with pool.Fori(0, 2) as i:
            for t in range(TT):
                pool.wait_ge(read[3], 17 + t + 1 + 4 * i)
                Q.tensor_tensor(OA[:, t, :], OA[:, t, :], OTMP[:], ADD).then_inc(S("oa_added"), 1)
        merge_sum("branch2", KT, H2 + KT)
        add_squares(2, 5, lambda j, i: (S("ysq_ready"), KT + j + 1 + 4 * i))
        add_squares(3, 6, lambda j, i: (S("ysq_ready"), 2 * KT + j + 1 + 4 * i))


    ctx.close()


_CONSTS = constants()
_OUT = (1, T, D)


def kernel(**inputs):
    import concourse.bacc as _bacc
    from concourse import mybir as _mybir
    from concourse.bass_utils import run_bass_kernel_spmd as _run

    nc = _bacc.Bacc("TRN2", target_bir_lowering=False, num_devices=1)
    arrays = {name: np.ascontiguousarray(v) for name, v in inputs.items()}
    arrays["rows"] = np.concatenate([np.asarray(inputs[name]).reshape(-1, P) for name, _ in ROWS])
    arrays.update(_CONSTS)
    aps = {}
    for name, v in arrays.items():
        aps[name] = nc.dram_tensor(f"in_{name}", v.shape, _mybir.dt.from_np(v.dtype), kind="ExternalInput").ap()
    out = nc.dram_tensor("out", _OUT, _mybir.dt.float32, kind="ExternalOutput").ap()
    build(nc, aps, out)
    r = _run(nc, [{f"in_{name}": v for name, v in arrays.items()}], core_ids=[0])
    return r.results[0]["out"]
```

```python
import numpy as np
import concourse.bass as bass
from concourse import mybir
from contextlib import ExitStack

P = 128
T = 512
D = 1024
KT = D // P
TT = T // P
POOL_G = 4
CONV_K = 31
CONV_C = 512
CC = CONV_C // P
EPS = 1e-6
SLAB = 256
HEADS, HD = 8, 64
N_CMP = 31
GLA_H, GLA_DK, GLA_DV = 4, 64, 128
SLC_LEN, SLC_TOPK, WINDOW = 64, 16, 512
assert T <= SLC_LEN * SLC_TOPK and T <= WINDOW
LEVELS = 7
KB = 1024

C2_Q, C2_KV, C2_GATE, C2_QG, C2_KG, C2_VG, C2_LR, C2_RG, C2_MG = 0, 512, 1280, 1304, 1560, 1816, 2328, 2344, 2856

ROWS = [("norm_mix_pre", 8), ("pool_scale", 4), ("conv_b", 4), ("conv_ln_g", 4), ("conv_ln_b", 4),
        ("norm_mix_post", 8), ("norm_mlp_pre", 8), ("norm_mlp_post", 8), ("norm_mix_2", 8),
        ("norm_ffn_2", 8), ("norm_final_2", 8), ("gla_norm_2", 1), ("gla_gate_b_2", 2),
        ("cmp_pe_k_2", 16), ("cmp_pe_v_2", 16)]
ROW0 = {}
_at = 0
for _name, _n in ROWS:
    ROW0[_name] = _at
    _at += _n
N_ROWS = _at


class Count:

    def __init__(self, sem):
        self.sem, self.n, self.extra = sem, 0, 0

    def inc(self, ins):
        self.n += 1
        ins.then_inc(self.sem, 1)

    def wait(self, eng, back=0):
        eng.wait_ge(self.sem, self.n - back + self.extra)

    def enter(self, i, per):
        self.extra, self.start, self.per = i * per, self.n, per

    def leave(self, times):
        assert self.n - self.start == self.per, (self.n - self.start, self.per)
        self.n, self.extra = self.start + self.per * times, 0


def constants():
    f = np.float32
    ident = np.eye(P, dtype=f)
    recip = np.zeros((P, POOL_G, 16), f)
    for g in range(POOL_G):
        recip[:, g, :] = (f(1) / np.minimum(np.arange(1, 17), 2 << g).astype(f))[None, :]
    half = 8
    inv_freq = f(500000.0) ** (-np.arange(half, dtype=f) / f(half))
    ang = np.arange(T, dtype=f)[None, :] * inv_freq[:, None].astype(f)
    cos, sin = np.ones((P, T), f), np.zeros((P, T), f)
    rot = np.zeros((P, P), f)
    for base in (0, HD):
        for k in range(half):
            cos[base + k] = cos[base + half + k] = np.cos(ang[k])
            sin[base + k] = sin[base + half + k] = np.sin(ang[k])
            rot[base + half + k, base + k] = -1.0
            rot[base + k, base + half + k] = 1.0
    causal = np.where(np.arange(P)[None, :] <= np.arange(P)[:, None], 0.0, -1e30).astype(f)
    cmp_mask = np.full((P, TT, 32), -1e30, f)
    for t in range(TT):
        for n in range(N_CMP):
            cmp_mask[:, t, n] = np.where(16 * n + 31 <= t * P + np.arange(P), 0.0, -1e30)
    level = np.zeros((P, LEVELS + 1, P), f)
    s, t = np.arange(P)[:, None], np.arange(P)[None, :]
    for l in range(LEVELS):
        h = 64 >> l
        level[:, l] = ((s // (2 * h) == t // (2 * h)) & (s % (2 * h) < h) & (t % (2 * h) >= h))
    level[:, LEVELS] = s == t
    reset = np.broadcast_to((np.arange(T) % P != 0).astype(f), (P, T))
    return {"c_ident": ident, "c_recip": recip.reshape(P, -1), "c_cos": cos, "c_sin": sin, "c_rot": rot,
            "c_causal": causal, "c_cmp_mask": cmp_mask.reshape(P, -1), "c_level": level.reshape(P, -1),
            "c_reset": np.ascontiguousarray(reset)}


def build(nc, a, out):
    f32, f32r, bf16 = mybir.dt.float32, mybir.dt.float32r, mybir.dt.bfloat16
    ALU, ACT, AX = mybir.AluOpType, mybir.ActivationFunctionType, mybir.AxisListType
    ADD, SUB, MUL, MAX = ALU.add, ALU.subtract, ALU.mult, ALU.max

    def at(name, shape, dt, kb):
        return nc.alloc_sbuf_tensor_at(name, [P] + shape, dt, offset=16512 + int(kb * KB))

    def f(ap):
        return ap.bitcast(f32)

    XT = at("x_T", [KT, T], f32, 0)
    HHI, HLO = at("h_hi", [KT, T], f32r, 16), at("h_lo", [KT, T], f32r, 32)
    RAW = [at(f"w_raw{i}", [KT, SLAB], f32, 48 + 8 * i) for i in range(2)]
    WHI = [at(f"w_hi{i}", [KT, SLAB], f32r, 64 + 8 * i) for i in range(2)]
    WLO = [at(f"w_lo{i}", [KT, SLAB], f32r, 80 + 8 * i) for i in range(2)]
    CB = 96
    IDENT = at("ident", [P], f32, CB)
    INV = {n: at(f"inv{n}", [P], f32, CB + 0.5 * (1 + j)) for j, n in enumerate((1024, 512, 128))}
    PV, CW = at("param_cols", [P], f32, CB + 2), at("conv_cols", [P], f32, CB + 2.5)
    RECIP = at("recip", [POOL_G, 16], f32, CB + 3)
    EPSB = at("eps", [1], f32, CB + 3.25)
    TMP16 = at("pool_head", [16], f32, CB + 3.375)
    ROT = at("rot", [P], f32, CB + 3.5)
    CAUS32, CAUSB = at("causal32", [P], f32, CB + 4), at("causal", [P], bf16, CB + 4.5)
    IDENTB = at("ident_b", [P], bf16, CB + 4.75)
    CMPM32, CMPMB = at("cmp_mask32", [TT, 32], f32, CB + 5), at("cmp_mask", [TT, 32], bf16, CB + 5.5)
    ROWS_T, CROWS_T = at("param_rows", [P], f32, CB + 6), at("conv_rows", [P], f32, CB + 6.5)
    W2G = at("gla_w2", [GLA_H * GLA_DK], f32, CB + 7)
    SB = 105
    SQ = [at(f"sq{i}", [T], f32, SB + 2 * i) for i in range(2)]
    HS = [at(f"h_now{i}", [T], f32, SB + 4 + 2 * i) for i in range(2)]
    SQA, RS, RSTD = (at(n, [T], f32, SB + 8 + 2 * j) for j, n in enumerate(("sq_sum", "root", "rstd")))
    R1 = 119.5
    GT = at("gate_tanh", [2 * KT, T], f32, R1)
    XTOK = at("x_tok", [TT, D], f32, R1)
    XSQ = at("x_tok_squares", [D], f32, R1 + 16)
    DIAG = at("rstd_diagonals", [TT, P], f32, R1 + 20)
    SUM4, ROOT4 = at("x_square_sums", [TT], f32, R1 + 22), at("x_rms", [TT], f32, R1 + 22.125)
    VP = at("v_padded", [CC, 30 + T], f32, R1 + 32)
    CV = at("conv_out", [CC, T], f32, R1 + 40.5)
    PHI, PLO = at("pool_hi", [POOL_G, T], f32r, R1 + 48.5), at("pool_lo", [POOL_G, T], f32r, R1 + 56.5)
    CHI, CLO = at("conv_hi", [CC, T], f32r, R1 + 64.5), at("conv_lo", [CC, T], f32r, R1 + 72.5)
    PLD = at("pooled", [POOL_G, T], f32, R1 + 64.5)
    UP = [at(f"u_padded{i}", [16 + T], f32, R1 + (72.5, 84.5)[i]) for i in range(2)]
    S2 = [at(f"window_sum{i}", [16 + T], f32, R1 + 74.75 + 2.25 * i) for i in range(2)]
    POOLW = at("pool_w_sb", [POOL_G, P], f32, R1 + 82)
    SG = [at(f"glu_tanh{i}", [T], f32, SB + 4 + 2 * i) for i in range(2)]
    Y = at("y_T", [KT, T], f32, R1 + 66)
    HN = at("h_T", [KT, T], f32, R1 + 66)
    FHI = [at(f"f_hi{i}", [KT, T], f32r, R1 + 32 * i) for i in range(2)]
    FLO = [at(f"f_lo{i}", [KT, T], f32r, R1 + 16 + 32 * i) for i in range(2)]
    RL = [at(f"relu{i}", [T], f32, SB + 4 + 2 * i) for i in range(2)]
    FF = [at(f"f_now{i}", [T], f32, SB + 2 * i) for i in range(2)]

    G = [nc.alloc_psum_tensor(f"gemm{i}", [P, T], f32) for i in range(4)]
    M = [nc.alloc_psum_tensor(f"misc{i}", [P, T], f32) for i in range(4)]

    ctx = ExitStack()
    sems = {}

    def S(name):
        if name not in sems:
            sems[name] = ctx.enter_context(nc.semaphore(name))
        return sems[name]

    raw_ready = [S("raw_ready0"), S("raw_ready1")]
    evac = [S(f"evacuated{i}") for i in range(4)]

    PH, s_at, b_at = {}, 0, 0
    for name, n, bps in [("in", 14, 2), ("branch", 4, 4), ("wo", 4, 2)] + \
            [("up0", 4, 2), ("up1", 4, 2), ("down0", 4, 2), ("up2", 4, 2), ("down1", 4, 2), ("up3", 4, 2),
             ("down2", 4, 2), ("down3", 4, 2)] + \
            [("small", 1, 1), ("gla", 6, 2), ("nsa", 5, 2), ("merge_b", 4, 2), ("merge_a", 4, 2), ("branch2", 4, 4), ("wout", 4, 2),
             ("fup0", 8, 2), ("fup1", 8, 2), ("fdown0", 4, 2), ("fup2", 6, 2), ("fdown1", 4, 2), ("fdown2", 4, 2)]:
        PH[name] = (s_at, n, b_at, bps)
        s_at, b_at = s_at + n, b_at + n * bps
    N_SLABS = s_at
    BLOCKS_BEFORE = []
    for s0, n, b0, bps in PH.values():
        BLOCKS_BEFORE += [b0 + j * bps for j in range(n)]
    BLOCKS_BEFORE.append(b_at)

    def evac_at(m, i=0, per=0):
        return evac[m % 4], m // 4 + 2 + i * (per // 4)

    def col(name, j=0, h=False):
        return PV[:, ROW0[name] + j:ROW0[name] + j + 1]

    def tiles(ap):
        return ap.rearrange("(k p) c -> p k c", p=P)

    w_in, w_po, w_co, w_o = (tiles(a[n][0]) for n in ("w_in", "w_pool_out", "w_conv_out", "w_o"))
    w_up, w_down = tiles(a["w_up"][0]), tiles(a["w_down"][0])
    ds = bass.ds

    block = ctx.enter_context(nc.Block())
    CONST_DMAS = 5

    ONEB, GTH, GATES = at("one", [1], f32, CB + 8), at("gate_tanh_small", [TT, 24], f32, CB + 8.125), at("gates", [TT, 24], f32, CB + 8.5)
    EL = at("gla_chunk_decay", [2, TT], f32, CB + 8.875)
    W1 = [at(f"cmp_w1_{i}", [16, P], f32, R1 + 8 * i) for i in range(2)]
    A = at("gla_attn", [GLA_H, T], f32, R1 + 16)
    OSB = at("gla_out", [GLA_H, T], f32, R1 + 16)
    RG = at("gla_gate", [GLA_H, T], f32, R1 + 24)
    QG, KG = at("q_gla", [2, T], f32, R1 + 32), at("k_gla", [2, T], f32, R1 + 36)
    VG = at("v_gla", [TT, GLA_H, GLA_DV], f32, R1 + 40)
    CUM, SMALL = at("log_decay", [2, T], f32, R1 + 48), at("lr_and_gates", [T], f32, R1 + 52)
    LEVM = at("level_masks", [LEVELS + 1, P], mybir.dt.uint8, R1 + 54)
    LEV32 = at("level_masks32", [LEVELS + 1, P], f32, R1 + 55)
    QL, KL = at("q_level", [2, T], f32, R1 + 55), at("k_level", [2, T], f32, R1 + 59)
    RESET = at("chunk_start", [T], f32, R1 + 59)
    RS4 = at("gla_roots", [T], f32, R1 + 55)
    ONE32 = at("one_32nd", [P], f32, CB + 6.5)
    ST = at("gla_state", [2, 3, GLA_DV], f32, R1 + 63)
    KTOK = at("k_tokens", [TT, GLA_H * GLA_DK], f32, SB + 4)
    VS = [at(f"v_stage{i}", [T], f32, SB + 10 + 2 * i) for i in range(2)]
    QR, QT = at("q_raw", [4, T], f32, R1 + 66), at("q_rope", [4, T], f32, R1 + 32)
    KR, VT = at("k_rope", [2, T], f32, R1 + 74), at("v_tokens", [2, TT, P], f32, R1 + 78)
    RAWC = at("kv_cmp_raw", [2, T], f32, R1 + 82)
    COS, SIN = at("cos", [T], f32, SB + 8), at("sin", [T], f32, R1 + 86)
    OBHI, OBLO = at("ob_hi", [4, T], f32r, R1 + 40), at("ob_lo", [4, T], f32r, R1 + 48)
    Z = at("cmp_windows", [4, T + 32], f32, R1 + 56)
    OA = at("oa_tokens", [TT, HEADS * HD], f32, R1 + 56)
    VBD = at("v_cmp_blocks", [2, 4 * HD], f32, R1 + 82)
    W2 = [at(f"cmp_w2_{i}", [HD], f32, CB + 6 + 0.25 * i) for i in range(2)]
    HX = [at(f"cmp_hidden{i}", [2 * 32], f32, R1 + 64.5 + 0.25 * i) for i in range(2)]
    HT = [at(f"cmp_tanh{i}", [2 * 32], f32, R1 + 65 + 0.25 * i) for i in range(2)]
    HB = at("cmp_bias", [2], f32, R1 + 65.5)
    KC = at("k_cmp", [32], f32, R1 + 65.625)
    KNOW = at("k_now", [T], f32, R1 + 84)
    PC, PCT = at("p_cmp", [TT, HEADS, 32], f32, SB), at("p_cmp_T", [2 * TT, P], f32, SB + 4)
    PB = [at(f"probs{i}", [2, T], f32, SB + 4 * i) for i in range(2)]
    PT = [at(f"probs_T{i}", [T], f32, SB + 8 + 2 * i) for i in range(2)]
    OTMP = at("o_scaled", [T], f32, SB + 12)
    MXC, SMC, FC = (at(n, [TT * HEADS], f32, R1 + 86 + 0.125 * j) for j, n in enumerate(("cmp_max", "cmp_sum", "cmp_factor")))
    NM = [at(f"row_max{i}", [2], f32, R1 + 86.5 + 0.0625 * i) for i in range(2)]
    NG = [at(f"neg_max{i}", [2], f32, R1 + 86.625 + 0.0625 * i) for i in range(2)]
    SUM = [at(f"row_sum{i}", [HEADS], f32, R1 + 86.75 + 0.0625 * i) for i in range(2)]
    FS = at("o_factor", [HEADS], f32, R1 + 86.875)
    OAHI, OALO = at("oa_hi", [4, T], f32r, R1 + 66), at("oa_lo", [4, T], f32r, R1 + 32)
    FG = [at(f"ffn_now{i}", [T], f32, R1 + 82 + 2 * i) for i in range(2)]
    OTK = at("out_tokens", [TT, D], f32, R1)

    read = [S(f"misc_read{i}") for i in range(4)]
    H2, F2 = 7 * KT, 4 * KT

    @block.sync
    def _(sp):
        for t in range(TT):
            sp.dma_start(XTOK[:, t, :], a["x"][0, t * P:(t + 1) * P, :]).then_inc(S(f"x_loaded{t}"), 16)

        def load(s, par, pieces, first=False):
            if not first:
                sp.wait_ge(S("lo_done"), s - 1)
            for dst, src in pieces:
                sp.dma_start(dst, src).then_inc(raw_ready[par], 16)

        def halves(par, w, k0, c0, kts=KT):
            h = kts // 2
            return [(RAW[par][:, 0:h, :], w[:, k0:k0 + h, ds(c0, SLAB)]),
                    (RAW[par][:, h:kts, :], w[:, k0 + h:k0 + kts, ds(c0, SLAB)])]

        def run(name, w, k0=0, c0=0, kts=KT):
            s0, n = PH[name][0:2]
            with sp.Fori(0, n // 2) as i:
                for j in range(2):
                    load(s0 + j + 2 * i, (s0 + j) % 2, halves((s0 + j) % 2, w, k0, c0 + SLAB * j + 2 * SLAB * i, kts))

        for c in range(CC):
            par = c % 2
            load(c, par, [(RAW[par][:, :, 0:P], w_in[:, :, 512 + c * P:512 + (c + 1) * P]),
                          (RAW[par][:, :, P:SLAB], w_in[:, :, 1024 + c * P:1024 + (c + 1) * P])], first=c < 2)
        for j in range(2):
            load(4 + j, j, halves(j, w_in, 0, SLAB * j))
        with sp.Fori(0, 4) as i:
            for j in range(2):
                load(6 + j + 2 * i, j, halves(j, w_in, 0, 1536 + SLAB * j + 2 * SLAB * i))
        s0 = PH["branch"][0]
        with sp.Fori(0, 2) as i:
            for j in range(2):
                load(s0 + j + 2 * i, j, [(RAW[j][:, 0:4, :], w_po[:, :, ds(SLAB * j + 2 * SLAB * i, SLAB)]),
                                         (RAW[j][:, 4:8, :], w_co[:, :, ds(SLAB * j + 2 * SLAB * i, SLAB)])])
        run("wo", w_o)
        for ch in range(4):
            run(f"up{ch}", w_up, c0=1024 * ch)
            if ch:
                run(f"down{ch - 1}", w_down, k0=KT * (ch - 1))
        run("down3", w_down, k0=KT * 3)
        w_2 = tiles(a["w_in_2"][0])
        s0 = PH["small"][0]
        load(s0, 0, [(RAW[0][:, :, 0:32], w_2[:, :, C2_LR:C2_LR + 32]),
                     (RAW[0][:, :, 32:P], w_2[:, :, C2_GATE:C2_GATE + 96])])
        for j, c0 in enumerate((C2_QG, C2_KG, C2_VG, C2_VG + SLAB, C2_RG, C2_RG + SLAB,
                                C2_KV, C2_KV + SLAB, C2_KV + 2 * SLAB)):
            load(s0 + 1 + j, (1 + j) % 2, halves((1 + j) % 2, w_2, 0, c0))
        for j in range(2):
            par = j % 2
            load(s0 + 10 + j, par, [(RAW[par][:, :, :].rearrange("p k (b g d) -> p k b g d", b=2, g=2)[:, :, b, g, :],
                                     w_2[:, :, g * 4 * HD + (2 * j + b) * HD:g * 4 * HD + (2 * j + b + 1) * HD])
                                    for b in range(2) for g in range(2)])
        run("merge_b", w_2, c0=C2_MG + D)
        run("merge_a", w_2, c0=C2_MG)
        w_ua, w_ub = tiles(a["w_up_nsa_2"][0]), tiles(a["w_up_gla_2"][0])
        s0 = PH["branch2"][0]
        with sp.Fori(0, 2) as i:
            for j in range(2):
                load(s0 + j + 2 * i, j, [(RAW[j][:, 0:4, :], w_ua[:, :, ds(SLAB * j + 2 * SLAB * i, SLAB)]),
                                         (RAW[j][:, 4:8, :], w_ub[:, :, ds(SLAB * j + 2 * SLAB * i, SLAB)])])
        run("wout", tiles(a["w_out_2"][0]))
        w_g, w_u, w_d = (tiles(a[n][0]) for n in ("w_ffn_gate_2", "w_ffn_up_2", "w_ffn_down_2"))

        def gate_up(name, c0):
            s0, n = PH[name][0:2]
            with sp.Fori(0, n // 2) as i:
                for j, w in enumerate((w_g, w_u)):
                    load(s0 + j + 2 * i, (s0 + j) % 2, halves((s0 + j) % 2, w, 0, c0 + SLAB * i))

        gate_up("fup0", 0)
        gate_up("fup1", 1024)
        run("fdown0", w_d)
        gate_up("fup2", 2048)
        run("fdown1", w_d, k0=KT)
        run("fdown2", w_d, k0=2 * KT, kts=6)
        for k in range(KT):
            sp.wait_ge(S("out_ready"), k + 1)
            sp.dma_start(out[0].rearrange("(t p) c -> p t c", p=P)[:, :, k * P:(k + 1) * P],
                         OTK[:, :, k * P:(k + 1) * P]).then_inc(S("stored"), 16)
        sp.wait_ge(S("stored"), 16 * KT)

    @block.tensor
    def _(pe):
        squares = Count(S("sq_used"))

        def gemm(bank, free, par, kts, col0, hi, lo, ready=None):
            pe.wait_ge(*free)
            first = True
            for n, kt in enumerate(kts):
                if ready:
                    ready(n)
                for w, x in ((WHI, hi), (WHI, lo), (WLO, hi)):
                    last = n == len(kts) - 1 and w is WLO
                    mm = nc.tensor.matmul(bank[:], w[par][:, kt, col0:col0 + P], x(n), start=first, stop=last)
                    first = False
            mm.then_inc(S("block_full"), 1)

        def slab(s, par, m, i, per, hi, lo, kts=range(KT), ready=None, blocks=2):
            pe.wait_ge(S("lo_done"), s + 1)
            for b in range(blocks):
                gemm(G[(m + b) % 4], (evac[(m + b) % 4], (m + b) // 4 + 1 + i * (per // 4)), par, kts, P * b, hi, lo,
                     ready if b == 0 else None)

        def h(t):
            return lambda n: t[:, n, :]

        def h_ready(base):
            return lambda n: pe.wait_ge(S("hlo_ready"), base + n + 1)

        def first_slab(s, blocks, hi_base, lo_base):
            par, m = s % 2, BLOCKS_BEFORE[s]
            pe.wait_ge(S("lo_done"), s + 1)
            for b in range(blocks):
                pe.wait_ge(evac[(m + b) % 4], (m + b) // 4 + 1)
            for k in range(KT):
                pe.wait_ge(S("hhi_ready"), hi_base + k + 1)
                for b in range(blocks):
                    for w in (WHI, WLO):
                        nc.tensor.matmul(G[(m + b) % 4][:], w[par][:, k, P * b:P * b + P], HHI[:, k, :],
                                         start=k == 0 and w is WHI, stop=False)
            for b in range(blocks):
                for k in range(KT):
                    pe.wait_ge(S("hlo_ready"), lo_base + k + 1)
                    mm = nc.tensor.matmul(G[(m + b) % 4][:], WHI[par][:, k, P * b:P * b + P], HLO[:, k, :],
                                          start=False, stop=k == KT - 1)
                mm.then_inc(S("block_full"), 1)

        def run(name, hi, lo, kts=range(KT), ready=None, lo_slab=0, slabs=None, new_h=None):
            s0, n, b0, bps = PH[name]
            n = slabs or n
            s0, b0 = s0 + lo_slab, b0 + lo_slab * bps
            if new_h:
                first_slab(s0, 2, *new_h)
                slab(s0 + 1, (s0 + 1) % 2, b0 + bps, 0, 0, hi, lo, kts)
                s0, b0, n = s0 + 2, b0 + 2 * bps, n - 2
            if n == 2:
                for j in range(2):
                    slab(s0 + j, (s0 + j) % 2, b0 + j * bps, 0, 0, hi, lo, kts, ready)
                return
            with pe.Fori(0, n // 2) as i:
                for j in range(2):
                    slab(s0 + j + 2 * i, (s0 + j) % 2, b0 + j * bps, i, 2 * bps, hi, lo, kts, ready)

        def mean_of_tiles(width, count, bank, ready_sem, base, done_sem, src=None):
            for k in range(count):
                if ready_sem:
                    pe.wait_ge(ready_sem, base + k + 1)
                x = src[:, k, :] if src is not None else SQ[k % 2][:]
                mm = nc.tensor.matmul(bank[:], INV[width][:], x, start=k == 0, stop=k == count - 1)
                if k < count - 1:
                    squares.inc(mm)
            mm.then_inc(done_sem, 1)

        def mean_of_sum(n, last):
            pe.wait_ge(S("sq_added"), KT * (n + 1))
            nc.tensor.matmul(M[0][:], INV[1024][:], SQA[:], start=True, stop=False)
            pe.wait_ge(*last)
            nc.tensor.matmul(M[0][:], INV[1024][:], SQ[1][:], start=False, stop=True).then_inc(S("mean_ready"), 1)

        pe.wait_ge(S("rows_loaded"), 48)
        nc.tensor.transpose(M[1][:, 0:N_ROWS], ROWS_T[0:N_ROWS, :], IDENT[0:N_ROWS, 0:N_ROWS]).then_inc(S("rows_transposed"), 1)
        nc.tensor.transpose(M[2][:, 0:CONV_K * CC], CROWS_T[0:CONV_K * CC, :], IDENT[0:CONV_K * CC, 0:CONV_K * CC]).then_inc(S("rows_transposed"), 1)
        for t in range(TT):
            pe.wait_ge(S(f"x_loaded{t}"), 16)
            for k in range(KT):
                if t == 0 and k == 5:
                    pe.wait_ge(S("cols_ready"), 2)
                mm = nc.tensor.transpose((G + M)[k][:, t * P:(t + 1) * P], XTOK[:, t, k * P:(k + 1) * P], IDENT[:])
                if t == TT - 1:
                    mm.then_inc(S("x_transposed"), 1)
        pe.wait_ge(S("inv_ready"), 1)
        pe.wait_ge(S("diagonals_ready"), 1)
        pe.wait_ge(S("x_upper"), 1)
        nc.tensor.matmul(M[0][:], INV[D][:], DIAG[:].rearrange("p t n -> p (t n)"), start=True, stop=True).then_inc(S("mean_ready"), 1)

        run("in", h(HHI), h(HLO), slabs=6, new_h=(0, 0))
        run("in", h(HHI), h(HLO), lo_slab=6, slabs=2)
        pe.wait_ge(S("pool_w_loaded"), 16)
        for g in range(POOL_G):
            pe.wait_ge(S("pooled_ready"), g + 1)
            nc.tensor.matmul(M[g][:], POOLW[:, g, :], PLD[:, g, :], start=True, stop=True).then_inc(S("mixed"), 1)
        run("in", h(HHI), h(HLO), lo_slab=8, slabs=2)
        slab(10, 0, 20, 0, 0, h(HHI), h(HLO))
        pe.wait_ge(S("pool_lo_ready"), POOL_G)
        mean_of_tiles(512, CC, M[0], None, 0, S("ln_mean"), src=CV)
        slab(11, 1, 22, 0, 0, h(HHI), h(HLO))
        mean_of_tiles(512, CC, M[1], S("lsq_ready"), 0, S("ln_var"), src=PLD)
        run("in", h(HHI), h(HLO), lo_slab=12, slabs=2)
        s0, _, b0, _ = PH["branch"]
        pe.wait_ge(S("clo_ready"), CC)
        with pe.Fori(0, 2) as i:
            for j in range(2):
                pe.wait_ge(S("lo_done"), s0 + j + 1 + 2 * i)
                for b in range(4):
                    hi, lo = ((PHI, PLO), (CHI, CLO))[b % 2]
                    m = b0 + 4 * j + b
                    gemm(G[m % 4], (evac[m % 4], m // 4 + 1 + 2 * i), j, range(4 * (b % 2), 4 * (b % 2) + 4),
                         P * (b // 2), h(hi), h(lo))
        hlo = KT
        run("wo", h(HHI), h(HLO), ready=h_ready(hlo))
        mean_of_sum(0, evac_at(PH["wo"][2] + KT - 1))
        mean_of_tiles(1024, KT, M[0], S("sq_ready"), 0, S("mean_ready"))
        hlo += KT
        for ch in range(4):
            run(f"up{ch}", h(HHI), h(HLO), new_h=(2 * KT, hlo) if ch == 0 else None)
            if ch:
                c = ch - 1
                run(f"down{c}", h(FHI[c % 2]), h(FLO[c % 2]), ready=h_ready(hlo + KT * (c + 1)))
        run("down3", h(FHI[1]), h(FLO[1]), ready=h_ready(hlo + KT * 4))
        mean_of_sum(1, (S("ysq_ready"), KT))
        mean_of_tiles(1024, KT, M[0], S("sq_ready"), KT, S("mean_ready"))
        misc = [Count(x) for x in read]

        def take(b):
            if misc[b].n or misc[b].extra:
                misc[b].wait(pe)
            misc[b].n += 1
            return M[b]

        hlo = H2
        s0, _, m0, _ = PH["small"]

        def plain(j):
            s = s0 + j
            slab(s, s % 2, BLOCKS_BEFORE[s], 0, 0, h(HHI), h(HLO))

        first_slab(s0, 1, 3 * KT, hlo)
        plain(1)
        pe.wait_ge(*evac_at(m0))
        b1 = take(1)
        for t in range(TT):
            mm = nc.tensor.transpose(b1[:, t * 64:t * 64 + 64], SMALL[0:64, t * P:(t + 1) * P], IDENT[0:64, 0:64])
        mm.then_inc(S("gates_T"), 1)
        for j in range(2):
            nc.tensor.matmul(take(2 + j)[:], W2G[0:16, j * P:(j + 1) * P], SMALL[0:16, :], start=True, stop=True).then_inc(S("decay_in"), 1)
        plain(2)
        plain(3)

        def to_tokens(src, bank, sem):
            for t in range(TT):
                mm = nc.tensor.transpose(bank[:, t * P:(t + 1) * P], src[:, t * P:(t + 1) * P], IDENT[:])
            mm.then_inc(S(sem), 1)

        def v_head(hd):
            pe.wait_ge(*evac_at(BLOCKS_BEFORE[s0 + 3] + hd))
            to_tokens(VS[hd % 2], take(hd), "v_T")

        plain(4)
        v_head(0)
        v_head(1)
        plain(5)
        v_head(2)
        v_head(3)
        plain(6)

        def level(l):
            ql, kl = (QL, KL) if l < LEVELS else (QG, KG)
            if l < LEVELS:
                pe.wait_ge(S("ql_ready"), 2 * (l + 1))
                pe.wait_ge(S("kl_ready"), 2 * (l + 1))
            for hd in range(GLA_H):
                bank, pp = take(hd), GLA_DK * (hd % 2)
                for c in range(TT):
                    mm = nc.tensor.matmul(bank[:, c * P:(c + 1) * P], kl[pp:pp + GLA_DK, hd // 2, c * P:(c + 1) * P],
                                          ql[pp:pp + GLA_DK, hd // 2, c * P:(c + 1) * P], start=True, stop=True)
                mm.then_inc(S("level_full"), 1)

        def half(j, b):
            s = s0 + j
            m = BLOCKS_BEFORE[s] + b
            if b == 0:
                pe.wait_ge(S("lo_done"), s + 1)
            gemm(G[m % 4], (evac[m % 4], m // 4 + 1), s % 2, range(KT), P * b, h(HHI), h(HLO))

        def v_branch(i):
            pe.wait_ge(*evac_at(BLOCKS_BEFORE[s0 + 7] + 3 + 2 * i))
            to_tokens(VS[i], take(0), "vb_T")

        def gate_block(x):
            half(12 + x // 2, x % 2)

        for k in range(8):
            if k < LEVELS:
                half(7 + k // 2, k % 2)
            if k == 4:
                v_branch(0)
            if k == 6:
                v_branch(1)
            level(k)
        half(10, 1)
        pe.wait_ge(S("kl_ready"), 2 * LEVELS + 2)
        for j in range(2):
            to_tokens(KL[:, j, :], take(j), "k_T")
        half(11, 0)
        misc[0].wait(pe)
        misc[1].wait(pe)
        for j in range(2):
            bank = take(2 + j)
            for c in range(3):
                for q in range(2):
                    hd = 2 * j + q
                    mm = nc.tensor.matmul(bank[q * 64:q * 64 + 64, c * P:(c + 1) * P], KTOK[:, c, hd * 64:hd * 64 + 64],
                                          VG[:, c, hd, :], start=True, stop=True)
            mm.then_inc(S("update_full"), 1)
        half(11, 1)
        misc[2].wait(pe)
        misc[3].wait(pe)
        pe.wait_ge(S("ql_ready"), 2 * LEVELS + 2)
        for hd in range(GLA_H):
            bank, pp = take(hd), GLA_DK * (hd % 2)
            for c in range(TT):
                cs = slice(c * P, (c + 1) * P)
                mm = nc.tensor.matmul(bank[:, cs], VG[:, c, hd, :], A[:, hd, cs], start=True, stop=c == 0)
                if c:
                    mm = nc.tensor.matmul(bank[:, cs], ST[pp:pp + 64, hd // 2, c - 1, :], QL[pp:pp + 64, hd // 2, cs],
                                          start=False, stop=True)
            mm.then_inc(S("gla_out_full"), 1)
        gate_block(0)
        gate_block(1)
        for hd in range(GLA_H):
            pe.wait_ge(S("gla_sq_ready"), hd + 1)
            bank = take(0) if hd == 0 else bank
            nc.tensor.matmul(bank[32 * hd:32 * hd + 32, :], INV[128][:, 0:32], SQ[hd % 2][:], start=True, stop=True).then_inc(S("gla_mean"), 1)
        gate_block(2)
        pe.wait_ge(S("gla_rstd"), 1)
        for hd in range(GLA_H):
            nc.tensor.matmul(take((hd + 1) % 4)[:], ONE32[32 * hd:32 * hd + 32, :], RS4[32 * hd:32 * hd + 32, :],
                             start=True, stop=True).then_inc(S("gla_rstd_full"), 1)
        gate_block(3)
        pe.wait_ge(*evac_at(BLOCKS_BEFORE[s0 + 11] + 1))
        for n in range(6):
            x = KR[:, n, :] if n < 2 else QR[:, n - 2, :]
            nc.tensor.matmul(take(n % 4)[:], ROT[:], x, start=True, stop=True).then_inc(S("rotated"), 1)
        gate_block(4)
        gate_block(5)
        pe.wait_ge(S("cmp_loaded"), 16 * 4)
        pe.wait_ge(S("windows_a"), 4)
        pe.wait_ge(S("windows_b"), 4)
        pe.wait_ge(S("positions"), 2)
        for kv in range(2):
            bank = take(2 + kv)
            for j in range(16):
                mm = nc.tensor.matmul(bank[:, 0:66].rearrange("p (g n) -> p g n", n=33), W1[kv][:, j, :],
                                      Z[:, 2 * kv:2 * kv + 2, 2 * j:2 * j + T + 1:16], start=j == 0, stop=j == 15)
            mm.then_inc(S("hidden_full"), 1)
        gate_block(6)
        pe.wait_ge(S("hidden_ready"), 1)
        bank = take(0)
        for g in range(2):
            mm = nc.tensor.matmul(bank[64 * g:64 * g + 64, 0:N_CMP], W2[0][:], HX[0][:, 32 * g:32 * g + N_CMP], start=True, stop=True)
        mm.then_inc(S("kc_full"), 1)
        pe.wait_ge(S("hidden_ready"), 2)
        bank = take(1)
        for g in range(2):
            mm = nc.tensor.matmul(bank[0:32, 64 * g:64 * g + 64], HX[1][:, 32 * g:32 * g + 32], W2[1][:], start=True, stop=True)
        mm.then_inc(S("vc_full"), 1)
        misc[0].wait(pe)
        pe.wait_ge(S("masks_ready"), 1)
        for g in range(2):
            bank = take(2 + g)
            nc.tensor.matmul(bank[:].rearrange("p (t h n) -> p t h n", h=4, n=32), IDENTB[:],
                             CMPMB[:].unsqueeze(2).broadcast_to([P, TT, 4, 32]), start=True, stop=False)
            for t in range(TT):
                for q in range(4):
                    o = P * t + 32 * q
                    mm = nc.tensor.matmul(bank[:, o:o + N_CMP], QR[64 * g:64 * g + 64, q, t * P:(t + 1) * P],
                                          KC[64 * g:64 * g + 64, 0:N_CMP], start=False, stop=t == TT - 1 and q == 3)
            mm.then_inc(S("cmp_scores"), 1)
        gate_block(7)
        pe.wait_ge(S("cmp_probs"), 2)
        for t in range(TT):
            bank = take(t // 2) if t % 2 == 0 else bank
            for g in range(2):
                mm = nc.tensor.transpose(bank[:, (2 * (t % 2) + g) * P:(2 * (t % 2) + g + 1) * P],
                                         PC[:].rearrange("p t h n -> p t (h n)")[:, t, P * g:P * (g + 1)], IDENT[:])
            mm.then_inc(S("probs_T_full"), 1)
        for t in range(TT):
            if t % 2 == 0:
                misc[t // 2].wait(pe)
            bank = take((2 + t) % 4)
            for g in range(2):
                mm = nc.tensor.matmul(bank[:, 256 * g:256 * g + 256], PCT[:, 2 * t + g, :], VBD[:, g, :], start=True, stop=True)
            mm.then_inc(S("cmp_out_full"), 1)
        sM, _, mM, _ = PH["merge_a"]

        def gate_matmuls(i, first, count):
            for x in range(first, first + count):
                bl, kt, n = x // 24, x % 24 // 3, x % 3
                m = mM + bl
                if x % 48 == 0:
                    pe.wait_ge(S("lo_done"), sM + bl // 2 + 1 + 2 * i)
                if x % 24 == 0:
                    pe.wait_ge(evac[m % 4], m // 4 + 1 + i)
                w, y = ((WHI, HHI), (WHI, HLO), (WLO, HHI))[n]
                mm = nc.tensor.matmul(G[m % 4][:], w[bl // 2][:, kt, P * (bl % 2):P * (bl % 2) + P], y[:, kt, :],
                                      start=x % 24 == 0, stop=x % 24 == 23)
                if x % 24 == 23:
                    mm.then_inc(S("block_full"), 1)

        def scores(step, g):
            t, q = step // 4, step % 4
            bank, w = take(g), t * P
            qs = QT[64 * g:64 * g + 64, q, w:w + P]
            nc.tensor.matmul(bank[:, w:w + P], IDENTB[:], CAUSB[:], start=True, stop=False)
            if t:
                nc.tensor.matmul(bank[:, 0:w], qs, KNOW[64 * g:64 * g + 64, 0:w], start=False, stop=False)
            nc.tensor.matmul(bank[:, w:w + P], qs, KNOW[64 * g:64 * g + 64, w:w + P], start=False, stop=True).then_inc(S("scores_full"), 1)

        def transpose_probs(step, g):
            t, q = step // 4, step % 4
            misc[g].wait(pe)
            bank = take(2)
            for kb in range(t + 1):
                mm = nc.tensor.transpose(bank[:, kb * P:(kb + 1) * P], PB[q % 2][:, g, kb * P:(kb + 1) * P], IDENT[:])
            mm.then_inc(S("probs_T_full"), 1)

        def values(i, step, g):
            t, q = step // 4, step % 4
            hd = 4 * g + q
            for kb in range(t + 1):
                mm = nc.tensor.matmul(M[3][:, hd * HD:(hd + 1) * HD], PT[g][:, kb * P:(kb + 1) * P],
                                      VT[:, ds(i, 1), kb, g * 64:g * 64 + 64][:, 0, :], start=kb == 0, stop=kb == t)
            mm.then_inc(S("pv_done"), 1)

        pe.wait_ge(S("ropes_ready"), 6)
        with pe.Fori(0, 2) as i:
            per = (16, 16, 32, 4)
            for b in range(4):
                misc[b].enter(i, per[b])
            pe.wait_ge(S("keys_moved"), i + 1)
            for g in range(2):
                scores(0, g)
            gate_matmuls(i, 0, 12)
            done = [12 + 72 * n // (8 * TT) for n in range(8 * TT + 1)]
            for step in range(4 * TT):
                for g in range(2):
                    transpose_probs(step, g)
                    if g:
                        if step % 4 == 0:
                            take(3)
                        values(i, step, 0)
                    if step < 4 * TT - 1:
                        scores(step + 1, g)
                    n = 2 * step + g
                    gate_matmuls(i, done[n], done[n + 1] - done[n])
                misc[2].wait(pe)
                values(i, step, 1)
            gate_matmuls(i, 84, 12)
            for b in range(4):
                misc[b].leave(2)
        pe.wait_ge(S("oa_added"), 2 * TT + 1)
        for k in range(4):
            bank = take(k)
            for t in range(TT):
                mm = nc.tensor.transpose(bank[:, t * P:(t + 1) * P], OA[:, t, k * P:(k + 1) * P], IDENT[:])
            mm.then_inc(S("oa_T"), 1)
        s0, _, b0, _ = PH["branch2"]
        for k in range(4):
            misc[k].wait(pe)
        with pe.Fori(0, 2) as i:
            for j in range(2):
                pe.wait_ge(S("lo_done"), s0 + j + 1 + 2 * i)
                for b in range(4):
                    hi, lo = ((OAHI, OALO), (OBHI, OBLO))[b % 2]
                    m = b0 + 4 * j + b
                    gemm(G[m % 4], (evac[m % 4], m // 4 + 1 + 2 * i), j, range(4 * (b % 2), 4 * (b % 2) + 4),
                         P * (b // 2), h(hi), h(lo))
        run("wout", h(HHI), h(HLO), ready=h_ready(H2 + KT))
        mean_of_sum(2, (S("ysq_ready"), 2 * KT))
        fbase = H2 + 3 * KT
        run("fup0", h(HHI), h(HLO), new_h=(5 * KT, H2 + 2 * KT))
        run("fup1", h(HHI), h(HLO))
        run("fdown0", h(FHI[0]), h(FLO[0]), ready=h_ready(fbase))
        run("fup2", h(HHI), h(HLO))
        run("fdown1", h(FHI[1]), h(FLO[1]), ready=h_ready(fbase + KT))
        run("fdown2", h(FHI[0]), h(FLO[0]), kts=range(6), ready=h_ready(fbase + 2 * KT))
        mean_of_sum(3, (S("ysq_ready"), 3 * KT))
        for k in range(KT):
            pe.wait_ge(S("hs_ready"), 4 * KT + k + 1)
            if k >= 4:
                pe.wait_ge(S("out_ready"), k - 3)
            bank = M[k % 4]
            for t in range(TT):
                mm = nc.tensor.transpose(bank[:, t * P:(t + 1) * P], HS[k % 2][:, t * P:(t + 1) * P], IDENT[:])
            mm.then_inc(S("out_T"), 1)

    @block.scalar
    def _(act):
        for dst, src in [(IDENT[:], a["c_ident"]), (ROWS_T[0:N_ROWS, :], a["rows"]),
                         (CROWS_T[0:CONV_K * CC, :], a["conv_w"][0].rearrange("k (c p) -> (k c) p", p=P))]:
            act.dma_start(dst, src).then_inc(S("rows_loaded"), 16)
        for dst, src in [(RECIP[:], a["c_recip"].rearrange("p (g n) -> p g n", n=16)),
                         (ROT[:], a["c_rot"]), (CAUS32[:], a["c_causal"]),
                         (CMPM32[:], a["c_cmp_mask"].rearrange("p (t n) -> p t n", n=32)),
                         (W2G[0:16, :], a["gla_gate_w2_2"][0])]:
            act.dma_start(dst, src).then_inc(S("consts_loaded"), 16)
        act.dma_start(POOLW[:], a["pool_w"][0].rearrange("g c d -> c g d")).then_inc(S("pool_w_loaded"), 16)

        root = Count(S("root_ready"))

        def split_hi(s, par, i=0, kts=KT):
            act.wait_ge(raw_ready[par], 32 * (s // 2 + 1 + i) + (32 if s >= PH["nsa"][0] + 3 else 0))
            if s >= 2:
                per = BLOCKS_BEFORE[s] - BLOCKS_BEFORE[s - 1]
                act.wait_ge(S("block_full"), BLOCKS_BEFORE[s - 1] + 2 * per * i)
            nc.scalar.activation(WHI[par][:, 0:kts, :], RAW[par][:, 0:kts, :], ACT.Copy).then_inc(S("hi_done"), 1)

        def full(m, i=0, per=0):
            act.wait_ge(S("block_full"), m + 1 + i * per)

        def squares(used, x_base):
            for k in range(KT):
                act.wait_ge(S("x_ready"), x_base + k + 1)
                if k >= 2:
                    act.wait_ge(S("sq_used"), used + k - 1)
                nc.scalar.activation(SQ[k % 2][:], XT[:, k, :], ACT.Square).then_inc(S("sq_ready"), 1)

        def take_root(bank, sem, value):
            act.wait_ge(sem, value)
            root.inc(nc.scalar.activation(RS[:], bank[:], ACT.Sqrt, bias=EPSB[:]))

        def h_hi(base):
            for k in range(KT):
                act.wait_ge(S("hs_ready"), base + k + 1)
                nc.scalar.activation(HHI[:, k, :], HN[:, k, :], ACT.Copy).then_inc(S("hhi_ready"), 1)

        def run(name, evacuate, lo_slab=0, slabs=None):
            s0, n, b0, bps = PH[name]
            n = slabs or n
            s0, b0 = s0 + lo_slab, b0 + lo_slab * bps
            with act.Fori(0, n // 2) as i:
                for j in range(2):
                    split_hi(s0 + j + 1, (s0 + j + 1) % 2, i)
                    for b in range(bps):
                        evacuate(bps * j + b, b0 + bps * j + b, i)

        act.wait_ge(S("eps_ready"), 1)
        for t in range(TT):
            act.wait_ge(S(f"x_loaded{t}"), 16)
            if t:
                act.wait_ge(S("x_squared"), t)
            nc.scalar.activation(XSQ[:], XTOK[:, t, :], ACT.Square, accum_out=SUM4[:, t:t + 1]).then_inc(S("x_squared"), 1)
        act.wait_ge(S("x_squared"), TT)
        root.inc(nc.scalar.activation(ROOT4[:], SUM4[:], ACT.Sqrt, scale=1.0 / D, bias=EPSB[:]))
        for k in range(4):
            act.wait_ge(S("x_transposed"), k + 1)
            nc.scalar.activation(XT[:, k, :], G[k][:], ACT.Copy).then_inc(evac[k], 1)
        split_hi(0, 0)
        h_hi(0)

        def merge_gate(j, m, i):
            full(m, i, 4)
            nc.scalar.activation(GT[:, j + (m - j - 12) + 4 * i, :], G[m % 4][:], ACT.Tanh, scale=0.5).then_inc(evac[m % 4], 1)

        for c in range(CC):
            split_hi(c + 1, (c + 1) % 2)
            m = 2 * c + 1
            full(m)
            if c >= 2:
                act.wait_ge(*evac_at(m - 5))
            nc.scalar.activation(SG[c % 2][:], G[m % 4][:], ACT.Tanh, scale=0.5).then_inc(evac[m % 4], 1)
        for j in range(2):
            split_hi(CC + j + 1, (CC + j + 1) % 2)
            for b in range(2):
                g, m = 2 * j + b, 2 * (CC + j) + b
                full(m)
                if g >= 2:
                    act.wait_ge(S("pooled_ready"), g - 1)
                elif g == 0:
                    act.wait_ge(S("pads_ready"), 3)
                nc.scalar.activation(UP[g % 2][:, 16:16 + T], G[m % 4][:], ACT.Copy).then_inc(evac[m % 4], 1)
        run("in", merge_gate, lo_slab=6, slabs=4)
        for g in range(POOL_G):
            act.wait_ge(S("mixed"), g + 1)
            nc.scalar.activation(PHI[:, g, :], M[g][:], ACT.Copy, scale=col("pool_scale", g)).then_inc(S("pool_hi_ready"), 1)

        def last_gates(s):
            for m in (2 * s, 2 * s + 1):
                full(m)
                nc.scalar.activation(GT[:, m - 12, :], G[m % 4][:], ACT.Tanh, scale=0.5).then_inc(evac[m % 4], 1)

        split_hi(11, 1)
        last_gates(10)
        split_hi(12, 0)
        for c in range(CC):
            act.wait_ge(S("centred"), c + 1)
            nc.scalar.activation(PLD[:, c, :], CV[:, c, :], ACT.Square).then_inc(S("lsq_ready"), 1)
        last_gates(11)
        split_hi(13, 1)
        take_root(M[1], S("ln_var"), 1)
        for c in range(CC):
            act.wait_ge(S("ln_ready"), c + 1)
            if c >= 2:
                act.wait_ge(S("silu_ready"), c - 1)
            nc.scalar.activation(SQ[c % 2][:], CV[:, c, :], ACT.Tanh, scale=0.5).then_inc(S("ln_tanh"), 1)
            if c >= 1:
                act.wait_ge(S("silu_ready"), c)
                nc.scalar.activation(CHI[:, c - 1, :], CV[:, c - 1, :], ACT.Copy, scale=0.5).then_inc(S("chi_ready"), 1)
        act.wait_ge(S("silu_ready"), CC)
        nc.scalar.activation(CHI[:, CC - 1, :], CV[:, CC - 1, :], ACT.Copy, scale=0.5).then_inc(S("chi_ready"), 1)
        last_gates(12)
        split_hi(14, 0)
        last_gates(13)
        def merged_hi(name, base, scale):
            s0, n, b0, bps = PH[name]
            with act.Fori(0, n // 2) as i:
                for j in range(2):
                    split_hi(s0 + j + 1, (s0 + j + 1) % 2, i)
                    for q in range(2):
                        k = 2 * j + q
                        act.wait_ge(S("merged_ready"), base + k + 1 + 4 * i)
                        nc.scalar.activation(HHI[:, k + 4 * i, :], HS[k % 2][:], ACT.Copy, scale=scale).then_inc(S("hhi_ready"), 1)

        merged_hi("branch", 0, 0.5)
        def copy_square(name):
            def evacuate(j, m, i):
                full(m, i, 4)
                nc.scalar.activation(Y[:, j + 4 * i, :], G[m % 4][:], ACT.Copy).then_inc(S("y_ready"), 1)
                act.wait_ge(S("sq_added"), max(j, 1) + 4 * i)
                nc.scalar.activation(SQ[j % 2][:], G[m % 4][:], ACT.Square).then_inc(evac[m % 4], 1)
            return evacuate

        run("wo", copy_square("wo"))
        take_root(M[0], S("mean_ready"), 2)
        squares(2 * (CC - 1), 0)
        take_root(M[0], S("mean_ready"), 3)
        h_hi(KT)
        def up_evac(ch):
            def evacuate(j, m, i):
                full(m, i, 4)
                r = ch * KT + j + 4 * i
                act.wait_ge(*evac_at(m - 2, i, 4))
                nc.scalar.activation(RL[j % 2][:], G[m % 4][:], ACT.Relu).then_inc(S("relu_ready"), 1)
                act.wait_ge(*evac_at(m, i, 4))
                nc.scalar.activation(FHI[ch % 2][:, j + 4 * i, :], FF[j % 2][:], ACT.Copy).then_inc(S("fhi_ready"), 1)
            return evacuate

        def nothing(j, m, i):
            pass

        def first_copy(j, m, i):
            full(m, i, 4)
            nc.scalar.activation(Y[:, j + 4 * i, :], G[m % 4][:], ACT.Copy).then_inc(evac[m % 4], 1)

        def last_square(base):
            def evacuate(j, m, i):
                act.wait_ge(*evac_at(m, i, 4))
                act.wait_ge(S("sq_added"), base + max(j, 1) + 4 * i)
                nc.scalar.activation(SQ[j % 2][:], Y[:, j + 4 * i, :], ACT.Square).then_inc(S("ysq_ready"), 1)
            return evacuate

        run("up0", up_evac(0))
        run("up1", up_evac(1))
        run("down0", first_copy)
        run("up2", up_evac(2))
        run("down1", nothing)
        run("up3", up_evac(3))
        run("down2", nothing)
        run("down3", last_square(KT))
        take_root(M[0], S("mean_ready"), 4)
        squares(2 * (CC - 1) + KT - 1, KT)
        take_root(M[0], S("mean_ready"), 5)
        h_hi(2 * KT)
        s0, _, m0, _ = PH["small"]
        A_, same = nc.scalar.activation, Count(S("scalar_step"))

        def split(j):
            split_hi(s0 + j, (s0 + j) % 2)

        def copy_out(m, dst, func=ACT.Copy, **kw):
            full(m)
            A_(dst, G[m % 4][:], func, **kw).then_inc(evac[m % 4], 1)

        split(1)
        copy_out(m0, SMALL[:])
        split(2)
        for j in range(2):
            copy_out(m0 + 1 + j, QG[:, j, :], scale=GLA_DK ** -0.5)
        act.wait_ge(S("gates_T"), 1)
        A_(GTH[:], M[1][:, 0:TT * 64].rearrange("p (t n) -> p t n", n=64)[:, :, 32:56], ACT.Tanh, scale=0.5).then_inc(read[1], 1)
        for j in range(2):
            act.wait_ge(read[2 + j], 1)
            same.inc(A_(SQ[j][:], QL[:, j, :], ACT.Abs))
        act.wait_ge(S("ones_ready"), 1)
        for j in range(2):
            same.wait(act, 1)
            same.inc(A_(SQ[j][:], SQ[j][:], ACT.Exp, scale=-1.0))
        for j in range(2):
            same.wait(act, 1 - j)
            A_(HS[j][:], SQ[j][:], ACT.Ln, bias=ONEB[:]).then_inc(S("softplus_ready"), 1)
        split(3)
        for j in range(2):
            copy_out(m0 + 3 + j, KG[:, j, :])
        split(4)
        for hd in range(2):
            copy_out(m0 + 5 + hd, VS[hd][:])
        split(5)

        def v_out(hd):
            act.wait_ge(S("v_T"), hd + 1)
            A_(VG[:, :, hd, :], M[hd][:].rearrange("p (c d) -> p c d", d=P), ACT.Copy).then_inc(read[hd], 1)

        for hd in range(2):
            v_out(hd)
        for hd in range(2):
            copy_out(m0 + 7 + hd, VS[hd][:])
        split(6)

        def r_out(hd):
            full(m0 + 9 + hd)
            A_(RG[:, hd, :], G[(m0 + 9 + hd) % 4][:], ACT.Tanh, scale=0.5).then_inc(S("r_tanh"), 1)

        r_out(0)
        r_out(1)
        v_out(2)
        v_out(3)
        split(7)
        r_out(2)
        r_out(3)

        def level(l):
            for j in range(2):
                act.wait_ge(S("dd_ready"), 2 * l + j + 1)
                same.inc(A_(HS[j][:], HS[j][:], ACT.Abs))
                same.wait(act)
                if l:
                    act.wait_ge(S("ql_ready"), 2 * l - 1 + j)
                    act.wait_ge(S("kl_ready"), 2 * l - 1 + j)
                A_(SQ[j][:], HS[j][:], ACT.Exp, scale=-1.0 / 16).then_inc(S("decay_ready"), 1)

        mk = BLOCKS_BEFORE[s0 + 7]
        dests = [RAWC[:, 0, :], RAWC[:, 1, :], KR[:, 0, :], VS[0][:], KR[:, 1, :], VS[1][:]] + [QR[:, q, :] for q in range(4)]
        split(8)
        level(0)
        for k in range(7):
            copy_out(mk + k, dests[k], scale=1.0 if k < 6 else HD ** -0.5)
            if k % 2:
                split(9 + k // 2)
            for i in range(2):
                if k == 4 + 2 * i:
                    act.wait_ge(S("vb_T"), i + 1)
                    A_(VT[:, i, :, :], M[0][:].rearrange("p (c d) -> p c d", d=P), ACT.Copy).then_inc(read[0], 1)
            if k < LEVELS - 1:
                level(k + 1)
        for j in range(2):
            act.wait_ge(S("ql_ready"), 2 * LEVELS - 1 + j)
            act.wait_ge(S("kl_ready"), 2 * LEVELS - 1 + j)
            A_(SQ[j][:], CUM[:, j, :], ACT.Exp, scale=1.0 / 16).then_inc(S("q_decay"), 1)
            A_(EL[:, j, :], CUM[:, j, P - 1:T:P], ACT.Exp, scale=1.0 / 16).then_inc(S("chunk_decay"), 1)
        for j in range(2):
            act.wait_ge(S("dd_ready"), 2 * LEVELS + j + 1)
            same.inc(A_(HS[j][:], HS[j][:], ACT.Abs))
            same.wait(act)
            act.wait_ge(S("ql_ready"), 2 * LEVELS + 1 + j)
            A_(SQ[j][:], HS[j][:], ACT.Exp, scale=-1.0 / 16).then_inc(S("decay_ready"), 1)

        def q_out(k):
            copy_out(mk + k, dests[k], scale=HD ** -0.5)

        def gate_out(x):
            m = BLOCKS_BEFORE[s0 + 12] + x
            copy_out(m, GT[:, KT + x, :], ACT.Tanh, scale=0.5)

        q_out(7)
        split(12)
        for j in range(2):
            act.wait_ge(S("k_T"), j + 1)
            A_(KTOK[:, :, j * P:(j + 1) * P], M[j][:].rearrange("p (c d) -> p c d", d=P), ACT.Copy).then_inc(read[j], 1)
        q_out(8)
        q_out(9)
        split(13)
        act.wait_ge(S("gla_out_full"), 4)
        for hd in range(GLA_H):
            A_(OSB[:, hd, :], M[hd][:], ACT.Copy).then_inc(read[hd], 1)
        for hd in range(GLA_H):
            act.wait_ge(read[hd], (13, 12, 12, 12)[hd])
            if hd >= 2:
                act.wait_ge(S("gla_mean"), hd - 1)
            A_(SQ[hd % 2][:], OSB[:, hd, :], ACT.Square).then_inc(S("gla_sq_ready"), 1)
        act.wait_ge(S("gla_mean"), GLA_H)
        A_(RS4[:], M[0][:], ACT.Sqrt, bias=EPSB[:]).then_inc(read[0], 1)
        split(14)
        for hd in range(GLA_H):
            act.wait_ge(S("ob_ready"), hd + 1)
            A_(OBHI[:, hd, :], OSB[:, hd, :], ACT.Copy, scale=0.5).then_inc(S("ob_hi_ready"), 1)
        act.wait_ge(S("ob_lo_ready"), 4)
        for n in range(4):
            kv, g = n // 2, n % 2
            A_(Z[64:128, n, 0:T - 1], RAWC[64 * g:64 * g + 64, kv, 1:T], ACT.Copy).then_inc(S("windows_b"), 1)
        for x in range(4):
            gate_out(x)
        split(15)
        for kv in range(2):
            act.wait_ge(read[2 + kv], 15)
            A_(HT[kv][:], HX[kv][:], ACT.Tanh, scale=0.5).then_inc(S("hidden_tanh"), 1)
        gate_out(4)
        gate_out(5)
        split(16)
        for g in range(2):
            act.wait_ge(read[2 + g], 16)
            x = PC[:, :, 4 * g:4 * g + 4, :]
            A_(x, x, ACT.Exp).then_inc(S("cmp_probs"), 1)
        for p in range(2):
            act.wait_ge(S("probs_T_full"), 2 * (p + 1))
            A_(PCT[:, 4 * p:4 * p + 4, :], M[p][:].rearrange("p (c d) -> p c d", d=P), ACT.Copy).then_inc(read[p], 1)
        gate_out(6)
        gate_out(7)
        sM, _, mM, _ = PH["merge_a"]
        act.wait_ge(S("ropes_ready"), 2)
        act.wait_ge(S("windows_a"), 4)
        A_(KNOW[:], KR[:, 0, :], ACT.Copy).then_inc(S("keys_moved"), 1)
        with act.Fori(0, 2) as i:
            def a_out(bl):
                m = mM + bl
                full(m, i, 4)
                A_(GT[:, bl + 4 * i, :], G[m % 4][:], ACT.Tanh, scale=0.5).then_inc(evac[m % 4], 1)

            for step in range(4 * TT):
                t, q = step // 4, step % 4
                w = (t + 1) * P
                for g in range(2):
                    act.wait_ge(S("neg_ready"), 2 * step + g + 1 + 32 * i)
                    act.wait_ge(S("probs_T_full"), 2 * step + 1 + g + 32 * i)
                    A_(PB[q % 2][:, g, 0:w], M[g][:, 0:w], ACT.Exp, bias=NG[q % 2][:, g:g + 1],
                       accum_out=SUM[t % 2][:, 4 * g + q:4 * g + q + 1]).then_inc(read[g], 1)
                if q == 0 and t % 2 == 0:
                    split_hi(sM + t // 2 + 1, (sM + t // 2 + 1) % 2, i)
                if q == 2 and t:
                    a_out(t - 1)
            act.wait_ge(S("keys_moved"), 1 + i)
            A_(KNOW[:], KR[:, 1, :], ACT.Copy).then_inc(S("keys_moved"), 1)
            a_out(3)
        for k in range(4):
            act.wait_ge(S("oa_T"), k + 1)
            A_(OAHI[:, k, :], M[k][:], ACT.Copy).then_inc(S("oa_hi_ready"), 1)
        merged_hi("branch2", KT, 0.5)

        def x_square(base):
            def evacuate(j, m, i):
                act.wait_ge(*evac_at(m, i, 4))
                act.wait_ge(S("sq_added"), base + max(j, 1) + 4 * i)
                A_(SQ[j % 2][:], XT[:, j + 4 * i, :], ACT.Square).then_inc(S("ysq_ready"), 1)
            return evacuate

        run("wout", x_square(2 * KT))
        take_root(M[0], S("mean_ready"), 6)
        h_hi(3 * KT)
        def gate_up(name, ch):
            s0, n, b0, _ = PH[name]
            with act.Fori(0, n // 2) as i:
                for j in range(2):
                    split_hi(s0 + j + 1, (s0 + j + 1) % 2, i)
                    for b in range(2):
                        m = b0 + 2 * j + b
                        if j == 0:
                            full(m, i, 4)
                            A_(SQ[b][:], G[m % 4][:], ACT.Tanh, scale=0.5).then_inc(S("ffn_tanh"), 1)
                        else:
                            act.wait_ge(*evac_at(m, i, 4))
                            A_(FHI[ch % 2][:, b + 2 * i, :], FG[b][:], ACT.Copy, scale=0.5).then_inc(S("fhi_ready"), 1)

        gate_up("fup0", 0)
        gate_up("fup1", 1)
        run("fdown0", nothing)
        gate_up("fup2", 2)
        run("fdown1", nothing)
        s0, _, b0, _ = PH["fdown2"]
        last = x_square(3 * KT)
        for j in range(4):
            if j < 3:
                split_hi(s0 + j + 1, (s0 + j + 1) % 2)
            for b in range(2):
                last(2 * j + b, b0 + 2 * j + b, 0)
        take_root(M[0], S("mean_ready"), 7)
        for k in range(KT):
            act.wait_ge(S("out_T"), k + 1)
            A_(OTK[:, :, k * P:(k + 1) * P], M[k % 4][:].rearrange("p (t d) -> p t d", d=P), ACT.Copy).then_inc(S("out_ready"), 1)

    @block.vector
    def _(dve):
        V = nc.vector
        V.memset(EPSB[:], EPS).then_inc(S("eps_ready"), 1)
        for n in (128, 512):
            V.memset(INV[n][:], 1.0 / n)
        V.memset(INV[1024][:], 1.0 / 1024).then_inc(S("inv_ready"), 1)
        rstd = Count(S("rstd_ready"))
        step = Count(S("vector_step"))

        def split_lo(s, par, i=0, kts=KT):
            dve.wait_ge(S("hi_done"), s + 1 + 2 * i)
            V.tensor_tensor(WLO[par][:, 0:kts, :], RAW[par][:, 0:kts, :], f(WHI[par][:, 0:kts, :]), SUB).then_inc(S("lo_done"), 1)

        def full(m, i=0, per=0):
            dve.wait_ge(S("block_full"), m + 1 + i * per)

        def invert(root_at, used=None):
            dve.wait_ge(S("root_ready"), root_at)
            if used:
                dve.wait_ge(*used)
            rstd.inc(V.reciprocal(RSTD[:], RS[:]))
            rstd.wait(dve)

        def h_lo(base, gain, hi_base=None):
            hi_base = base if hi_base is None else hi_base
            """h = x gain / rms in two float32r parts."""
            for k in range(KT):
                V.scalar_tensor_tensor(HN[:, k, :], XT[:, k, :], col(gain, k), RSTD[:], MUL, MUL).then_inc(S("hs_ready"), 1)
            for k in range(KT):
                dve.wait_ge(S("hhi_ready"), hi_base + k + 1)
                V.tensor_tensor(HLO[:, k, :], HN[:, k, :], f(HHI[:, k, :]), SUB).then_inc(S("hlo_ready"), 1)

        def residual(gain):
            for k in range(KT):
                V.scalar_tensor_tensor(Y[:, k, :], Y[:, k, :], col(gain, k), RSTD[:], MUL, MUL).then_inc(S("y_scaled"), 1)
                if k:
                    dve.wait_ge(S("y_scaled"), scaled[0] + k)
                    V.tensor_tensor(XT[:, k - 1, :], XT[:, k - 1, :], Y[:, k - 1, :], ADD).then_inc(S("x_ready"), 1)
            dve.wait_ge(S("y_scaled"), scaled[0] + KT)
            V.tensor_tensor(XT[:, KT - 1, :], XT[:, KT - 1, :], Y[:, KT - 1, :], ADD).then_inc(S("x_ready"), 1)
            scaled[0] += KT

        scaled = [0]

        def run(name, evacuate, lo_slab=0, slabs=None):
            s0, n, b0, bps = PH[name]
            n = slabs or n
            s0, b0 = s0 + lo_slab, b0 + lo_slab * bps
            with dve.Fori(0, n // 2) as i:
                for j in range(2):
                    split_lo(s0 + j + 1, (s0 + j + 1) % 2, i)
                    for b in range(bps):
                        evacuate(bps * j + b, b0 + bps * j + b, i)

        dve.wait_ge(S("rows_transposed"), 2)
        V.tensor_copy(PV[:, 0:N_ROWS], M[1][:, 0:N_ROWS]).then_inc(S("cols_ready"), 1)
        V.tensor_scalar(CW[:, 0:CONV_K * CC], M[2][:, 0:CONV_K * CC], 0.5, None, MUL).then_inc(S("cols_ready"), 1)
        for k in range(4, KT):
            dve.wait_ge(S("x_transposed"), k + 1)
            V.tensor_copy(XT[:, k, :], M[k - 4][:]).then_inc(S("x_upper"), 1)
        dve.wait_ge(S("root_ready"), 1)
        dve.wait_ge(S("rows_loaded"), 48)
        step.inc(V.reciprocal(ROOT4[:], ROOT4[:]))
        step.wait(dve)
        V.scalar_tensor_tensor(DIAG[:], IDENT[:].unsqueeze(1).broadcast_to([P, TT, P]), float(D),
                               ROOT4[:].unsqueeze(2).broadcast_to([P, TT, P]), MUL, MUL).then_inc(S("diagonals_ready"), 1)
        dve.wait_ge(S("mean_ready"), 1)
        rstd.inc(V.tensor_copy(RSTD[:], M[0][:]))
        rstd.wait(dve)
        dve.wait_ge(S("cols_ready"), 2)
        for k in range(4):
            dve.wait_ge(evac[k], 1)
        dve.wait_ge(S("x_upper"), 4)
        h_lo(0, "norm_mix_pre")
        dve.wait_ge(S("consts_loaded"), CONST_DMAS * 16)
        V.tensor_copy(IDENTB[:], IDENT[:])
        V.tensor_copy(CAUSB[:], CAUS32[:])
        V.tensor_copy(CMPMB[:], CMPM32[:]).then_inc(S("masks_ready"), 1)
        dve.wait_ge(S("lo_done"), 1)

        def tap(c, k, back=0):
            x, w, y = VP[:, c, k:k + T], CW[:, k * CC + c:k * CC + c + 1], CV[:, c, :]
            if k == 0:
                dve.wait_ge(*evac_at(2 * c))
                step.inc(V.tensor_scalar(y, x, w, col("conv_b", c), MUL, ADD))
            else:
                step.wait(dve, back)
                step.inc(V.scalar_tensor_tensor(y, x, w, y, MUL, ADD))

        def conv(c, first, last):
            for k in range(first, last):
                tap(c, k)

        def glu(c):
            m = 2 * c
            dve.wait_ge(*evac_at(m + 1))
            V.scalar_tensor_tensor(VP[:, c, 30:30 + T], SG[c % 2][:], 1.0, G[m % 4][:], ADD, MUL).then_inc(evac[m % 4], 1)

        dve.wait_ge(S("pads_ready"), 3)
        glu(0)
        conv(0, 0, 12)
        glu(1)
        conv(0, 12, 26)
        glu(2)
        conv(0, 26, CONV_K)
        conv(1, 0, 8)
        glu(3)

        def pooled(g):
            dve.wait_ge(S("window_summed"), g + 1)
            total, u, w = S2[g % 2], UP[g % 2], 2 << g
            V.scalar_tensor_tensor(PLD[:, g, 16:T], total[:, 32:16 + T], 1.0 / w, u[:, 32:16 + T], MUL, SUB)
            if g:
                dve.wait_ge(S("pooled_ready"), g)
            step.inc(V.tensor_tensor(TMP16[:], total[:, 16:32], RECIP[:, g, :], MUL))
            step.wait(dve)
            V.tensor_tensor(PLD[:, g, 0:16], TMP16[:], u[:, 16:32], SUB).then_inc(S("pooled_ready"), 1)

        pooled(0)
        pooled(1)
        conv(1, 8, 20)
        pooled(2)
        conv(1, 20, CONV_K)
        pooled(3)
        for k in range(CONV_K):
            tap(2, k, 1)
            tap(3, k, 1)
        step.wait(dve)
        for g in range(POOL_G):
            dve.wait_ge(S("pool_hi_ready"), g + 1)
            V.scalar_tensor_tensor(PLO[:, g, :], M[g][:], col("pool_scale", g), f(PHI[:, g, :]), MUL, SUB).then_inc(S("pool_lo_ready"), 1)
        dve.wait_ge(S("ln_mean"), 1)
        for c in range(CC):
            V.tensor_tensor(CV[:, c, :], CV[:, c, :], M[0][:], SUB).then_inc(S("centred"), 1)
        invert(2, (S("hs_ready"), KT))
        dve.wait_ge(S("centred"), CC)
        dve.wait_ge(S("lsq_ready"), CC)
        for c in range(CC):
            step.inc(V.tensor_tensor(CV[:, c, :], CV[:, c, :], RSTD[:], MUL))
        for c in range(CC):
            step.wait(dve, CC - 1 - c)
            V.tensor_scalar(CV[:, c, :], CV[:, c, :], col("conv_ln_g", c), col("conv_ln_b", c), MUL, ADD).then_inc(S("ln_ready"), 1)
        for c in range(CC):
            dve.wait_ge(S("ln_tanh"), c + 1)
            V.scalar_tensor_tensor(CV[:, c, :], SQ[c % 2][:], 1.0, CV[:, c, :], ADD, MUL).then_inc(S("silu_ready"), 1)
            if c:
                dve.wait_ge(S("chi_ready"), c)
                V.scalar_tensor_tensor(CLO[:, c - 1, :], CV[:, c - 1, :], 0.5, f(CHI[:, c - 1, :]), MUL, SUB).then_inc(S("clo_ready"), 1)
        dve.wait_ge(S("chi_ready"), CC)
        V.scalar_tensor_tensor(CLO[:, CC - 1, :], CV[:, CC - 1, :], 0.5, f(CHI[:, CC - 1, :]), MUL, SUB).then_inc(S("clo_ready"), 1)
        dve.wait_ge(S("lo_done"), 15)
        def merge(name, hi_base, scale):
            s0, n, b0, bps = PH[name]
            with dve.Fori(0, n // 2) as i:
                for j in range(2):
                    split_lo(s0 + j + 1, (s0 + j + 1) % 2, i)
                    for q in range(2):
                        k = 2 * j + q
                        for side in range(2):
                            m = b0 + 4 * j + 2 * q + side
                            full(m, i, 8)
                            gt = GT[:, k + 4 * i + KT * side, :]
                            V.scalar_tensor_tensor(gt, gt, 1.0, G[m % 4][:], ADD, MUL).then_inc(evac[m % 4], 1)
                    for q in range(2):
                        k = 2 * j + q
                        dve.wait_ge(S("hhi_ready"), hi_base + k + 1 + 4 * i)
                        V.scalar_tensor_tensor(HLO[:, k + 4 * i, :], HS[k % 2][:], scale, f(HHI[:, k + 4 * i, :]), MUL, SUB).then_inc(S("hlo_ready"), 1)

        merge("branch", KT, 0.5)
        def nothing(j, m, i):
            pass

        run("wo", nothing)
        invert(3, (S("silu_ready"), CC))
        dve.wait_ge(S("y_ready"), KT)
        residual("norm_mix_post")
        invert(4, (S("y_scaled"), KT))
        h_lo(2 * KT, "norm_mlp_pre")
        def up_evac(ch):
            def evacuate(j, m, i):
                r = ch * KT + j + 4 * i
                dve.wait_ge(S("relu_ready"), r + 1)
                dve.wait_ge(S("hlo_ready"), 3 * KT + r)
                V.tensor_tensor(FF[j % 2][:], RL[j % 2][:], G[m % 4][:], MUL).then_inc(evac[m % 4], 1)
                dve.wait_ge(S("fhi_ready"), r + 1)
                V.tensor_tensor(FLO[ch % 2][:, j + 4 * i, :], FF[j % 2][:], f(FHI[ch % 2][:, j + 4 * i, :]), SUB).then_inc(S("hlo_ready"), 1)
            return evacuate

        def add_block(j, m, i):
            full(m, i, 4)
            y = Y[:, j + 4 * i, :]
            V.tensor_tensor(y, y, G[m % 4][:], ADD).then_inc(evac[m % 4], 1)

        run("up0", up_evac(0))
        run("up1", up_evac(1))
        run("down0", nothing)
        run("up2", up_evac(2))
        run("down1", add_block)
        run("up3", up_evac(3))
        run("down2", add_block)
        run("down3", add_block)
        invert(5, (S("hs_ready"), 2 * KT))
        dve.wait_ge(S("ysq_ready"), KT)
        residual("norm_mlp_post")
        invert(6, (S("y_scaled"), 2 * KT))
        h_lo(7 * KT, "norm_mix_2", 3 * KT)
        s0, _, m0, _ = PH["small"]

        def split(j):
            split_lo(s0 + j, (s0 + j) % 2)

        def chunks(ap, n=P):
            return ap.rearrange("p (c n) -> p c n", n=n)

        split(1)
        split(2)
        dve.wait_ge(read[1], 1)
        V.tensor_scalar(GATES[:], GTH[:], 0.5, 0.5, MUL, ADD).then_inc(S("gates_ready"), 1)
        dve.wait_ge(S("masks_small"), 1)
        for j in range(2):
            dve.wait_ge(S("decay_in"), j + 1)
            V.tensor_scalar(QL[:, j, :], M[2 + j][:], col("gla_gate_b_2", j), None, ADD).then_inc(read[2 + j], 1)
        dve.wait_ge(S("gla_consts"), 32)
        for j in range(2):
            dve.wait_ge(S("softplus_ready"), j + 1)
            step.inc(V.scalar_tensor_tensor(QL[:, j, :], QL[:, j, :], 0.0, HS[j][:], ALU.min, SUB))
            step.wait(dve)
            V.tensor_tensor_scan(CUM[:, j, :], RESET[:], QL[:, j, :], 0.0, MUL, ADD).then_inc(S("cum_ready"), 1)
        for j in range(3, 7):
            split(j)

        def r_gate(hd):
            m = m0 + 9 + hd
            dve.wait_ge(S("r_tanh"), hd + 1)
            V.scalar_tensor_tensor(RG[:, hd, :], RG[:, hd, :], 1.0, G[m % 4][:], ADD, MUL).then_inc(evac[m % 4], 1)

        r_gate(0)
        r_gate(1)
        split(7)
        r_gate(2)
        r_gate(3)

        def distance(l):
            n = P >> l if l < LEVELS else P
            at_ = n // 2 - 1 if l < LEVELS else P - 1
            for j in range(2):
                dve.wait_ge(S("cum_ready"), 2)
                if l:
                    dve.wait_ge(S("decay_ready"), 2 * l - 1 + j)
                c = chunks(CUM[:, j, :], n)
                V.tensor_tensor(chunks(HS[j][:], n), c, c[:, :, at_:at_ + 1].broadcast_to([P, T // n, n]), SUB).then_inc(S("dd_ready"), 1)

        def decayed_q(l):
            for j in range(2):
                dve.wait_ge(S("decay_ready"), 2 * l + j + 1)
                if l:
                    dve.wait_ge(S("level_full"), 4 * l)
                V.tensor_tensor(QL[:, j, :], QG[:, j, :], SQ[j][:], MUL).then_inc(S("ql_ready"), 1)

        def pick(l):
            for hd in range(GLA_H):
                dve.wait_ge(S("level_full"), 4 * l + hd + 1)
                V.copy_predicated(chunks(A[:, hd, :]), LEVM[:, l:l + 1, :].broadcast_to([P, TT, P]), chunks(M[hd][:])).then_inc(read[hd], 1)

        dve.wait_ge(S("attn_zero"), 1)
        distance(0)
        for k in range(8):
            if k % 2 == 0:
                split(8 + k // 2)
            if k < LEVELS:
                decayed_q(k)
                if k + 1 < LEVELS:
                    distance(k + 1)
            pick(k)
        for j in range(2):
            dve.wait_ge(S("q_decay"), j + 1)
            V.tensor_tensor(QL[:, j, :], QG[:, j, :], SQ[j][:], MUL).then_inc(S("ql_ready"), 1)
        distance(LEVELS)
        split(12)
        dve.wait_ge(S("chunk_decay"), 2)
        for j in range(2):
            dve.wait_ge(S("update_full"), j + 1)
            u = M[2 + j]
            step.inc(V.tensor_copy(ST[:, j, 0, :], u[:, 0:P]))
            step.wait(dve)
            step.inc(V.scalar_tensor_tensor(ST[:, j, 1, :], ST[:, j, 0, :], EL[:, j, 1:2], u[:, P:2 * P], MUL, ADD))
            step.wait(dve)
            V.scalar_tensor_tensor(ST[:, j, 2, :], ST[:, j, 1, :], EL[:, j, 2:3], u[:, 2 * P:3 * P], MUL, ADD).then_inc(read[2 + j], 1)
        split(13)
        step.inc(V.memset(ONE32[:], 1.0 / 32))
        dve.wait_ge(read[0], 14)
        step.wait(dve)
        V.reciprocal(RS4[:], RS4[:]).then_inc(S("gla_rstd"), 1)
        for hd in range(GLA_H):
            b = (hd + 1) % 4
            dve.wait_ge(S("gla_rstd_full"), hd + 1)
            V.scalar_tensor_tensor(OSB[:, hd, :], OSB[:, hd, :], col("gla_norm_2"), M[b][:], MUL, MUL).then_inc(read[b], 1)
            dve.wait_ge(read[b], (15, 13, 13, 13)[b])
            V.tensor_tensor(OSB[:, hd, :], OSB[:, hd, :], RG[:, hd, :], MUL).then_inc(S("ob_ready"), 1)
        for hd in range(GLA_H):
            dve.wait_ge(S("ob_hi_ready"), hd + 1)
            V.scalar_tensor_tensor(OBLO[:, hd, :], OSB[:, hd, :], 0.5, f(OBHI[:, hd, :]), MUL, SUB).then_inc(S("ob_lo_ready"), 1)
        split(14)
        dve.wait_ge(S("rope_loaded"), 32)
        for n in range(6):
            dst = KR[:, n, :] if n < 2 else QT[:, n - 2, :]
            dve.wait_ge(S("rotated"), n + 1)
            if n >= 2:
                dve.wait_ge(S("ropes_ready"), n - 1)
            V.tensor_tensor(SQ[n % 2][:], M[n % 4][:], SIN[:], MUL).then_inc(read[n % 4], 1)
            dve.wait_ge(S("cos_ready"), n + 1)
            dve.wait_ge(read[n % 4], (16, 14, 14, 14, 17, 15)[n])
            V.tensor_tensor(dst, SQ[n % 2][:], HS[n % 2][:], ADD).then_inc(S("ropes_ready"), 1)
        for n in range(4):
            kv, g = n // 2, n % 2
            V.tensor_copy(Z[0:64, n, 0:T], RAWC[64 * g:64 * g + 64, kv, :]).then_inc(S("windows_a"), 1)
        for kv in range(2):
            step.inc(V.memset(HX[kv][:], 0.0))
        split(15)
        for kv in range(2):
            u = M[2 + kv]
            dve.wait_ge(S("hidden_full"), kv + 1)
            step.inc(V.tensor_copy(HB[:, kv:kv + 1], u[:, 32:33]))
            step.wait(dve)
            V.tensor_scalar(chunks(HX[kv][:], 32)[:, :, 0:N_CMP], chunks(u[:, 0:66], 33)[:, :, 0:N_CMP],
                            HB[:, kv:kv + 1], None, ADD).then_inc(read[2 + kv], 1)
        for kv in range(2):
            dve.wait_ge(S("hidden_tanh"), kv + 1)
            V.scalar_tensor_tensor(HX[kv][:], HT[kv][:], 1.0, HX[kv][:], ADD, MUL).then_inc(S("hidden_ready"), 1)
        dve.wait_ge(S("kc_full"), 1)
        V.tensor_scalar(KC[:, 0:N_CMP], M[0][:, 0:N_CMP], 0.5, None, MUL).then_inc(read[0], 1)
        dve.wait_ge(S("vc_full"), 1)
        dve.wait_ge(S("blocks_zero"), 1)
        for g in range(2):
            for q in range(4):
                ins = V.tensor_scalar(VBD[32 * q:32 * q + 32, g, HD * q:HD * q + HD], M[1][0:32, HD * g:HD * g + HD], 0.5, None, MUL)
        ins.then_inc(read[1], 1)
        for g in range(2):
            x = M[2 + g][:].rearrange("p (t h n) -> p t h n", h=4, n=32)
            mx = MXC[:, 16 * g:16 * g + 16].rearrange("p (t h) -> p t h", h=4)
            dve.wait_ge(S("cmp_scores"), g + 1)
            step.inc(V.reduce_max(mx, x, AX.X))
            step.wait(dve)
            step.inc(V.tensor_scalar(mx, mx, -1e29, None, MAX))
            step.wait(dve)
            V.tensor_tensor(PC[:, :, 4 * g:4 * g + 4, :], x, mx.unsqueeze(3).broadcast_to([P, TT, 4, 32]), SUB).then_inc(read[2 + g], 1)
        for g in range(2):
            sm = SMC[:, 16 * g:16 * g + 16].rearrange("p (t h) -> p t h", h=4)
            dve.wait_ge(S("cmp_probs"), g + 1)
            step.inc(V.reduce_sum(sm, PC[:, :, 4 * g:4 * g + 4, :], AX.X))
            step.wait(dve)
            step.inc(V.tensor_scalar(sm, sm, 1e-30, None, MAX))
            step.wait(dve)
            step.inc(V.reciprocal(sm, sm))
            step.wait(dve)
            step.inc(V.tensor_tensor(FC[:].rearrange("p (t h) -> p t h", h=HEADS)[:, :, 4 * g:4 * g + 4], sm,
                                     GATES[:, :, 12 * g:12 * g + 12:3], MUL))
        split(16)
        step.wait(dve)
        for t in range(TT):
            dve.wait_ge(S("cmp_out_full"), t + 1)
            b = (2 + t) % 4
            V.tensor_tensor(chunks(OA[:, t, :], HD), chunks(M[b][:], HD),
                            FC[:, 8 * t:8 * t + 8].unsqueeze(2).broadcast_to([P, HEADS, HD]), MUL).then_inc(read[b], 1)
        with dve.Fori(0, 2) as i:
            step.enter(i, 2 * 16 + 2 * TT)

            def row_max(s, g):
                q = s % 4
                dve.wait_ge(S("scores_full"), 2 * s + g + 1 + 32 * i)
                step.inc(V.reduce_max(NM[q % 2][:, g:g + 1], M[g][:, 0:(s // 4 + 1) * P], AX.X))
                step.wait(dve)
                V.tensor_scalar(NG[q % 2][:, g:g + 1], NM[q % 2][:, g:g + 1], -1.0, None, MUL).then_inc(S("neg_ready"), 1)

            row_max(0, 0)
            row_max(0, 1)
            for s in range(4 * TT):
                t, w = s // 4, (s // 4 + 1) * P
                for g in range(2):
                    dve.wait_ge(S("probs_T_full"), 4 + 2 * s + g + 1 + 32 * i)
                    V.tensor_copy(PT[g][:, 0:w], M[2][:, 0:w]).then_inc(read[2], 1)
                    if s < 4 * TT - 1:
                        row_max(s + 1, g)
                if s % 4 < 3:
                    continue
                dve.wait_ge(S("pv_done"), 8 * (t + 1) + 32 * i)
                step.inc(V.reciprocal(FS[:], SUM[t % 2][:]))
                step.wait(dve)
                step.inc(V.tensor_tensor(FS[:], FS[:], GATES[:, t, ds(1 + i, HEADS, step=3)], MUL))
                step.wait(dve)
                dve.wait_ge(S("oa_added"), t + 1 + 4 * i)
                V.tensor_tensor(chunks(OTMP[:], HD), chunks(M[3][:], HD),
                                FS[:].unsqueeze(2).broadcast_to([P, HEADS, HD]), MUL).then_inc(read[3], 1)
            step.leave(2)
        for k in range(4):
            dve.wait_ge(S("oa_hi_ready"), k + 1)
            V.tensor_tensor(OALO[:, k, :], M[k][:], f(OAHI[:, k, :]), SUB).then_inc(read[k], 1)
        merge("branch2", 4 * KT, 0.5)

        def add_to_x(j, m, i):
            full(m, i, 4)
            x = XT[:, j + 4 * i, :]
            V.tensor_tensor(x, x, G[m % 4][:], ADD).then_inc(evac[m % 4], 1)

        run("wout", add_to_x)
        invert(7, (S("hs_ready"), 3 * KT))
        h_lo(H2 + 2 * KT, "norm_ffn_2", 5 * KT)
        fbase = H2 + 3 * KT

        def gate_up(name, ch):
            s0, n, b0, _ = PH[name]
            with dve.Fori(0, n // 2) as i:
                for j in range(2):
                    split_lo(s0 + j + 1, (s0 + j + 1) % 2, i)
                    for b in range(2):
                        m = b0 + 2 * j + b
                        if j == 0:
                            dve.wait_ge(S("ffn_tanh"), KT * ch + b + 1 + 2 * i)
                            dve.wait_ge(*evac_at(m - 2, i, 4))
                            V.scalar_tensor_tensor(HS[b][:], SQ[b][:], 1.0, G[m % 4][:], ADD, MUL).then_inc(evac[m % 4], 1)
                        else:
                            k = KT * ch + b
                            full(m, i, 4)
                            dve.wait_ge(*evac_at(m - 2, i, 4))
                            dve.wait_ge(S("hlo_ready"), fbase + k - 1 + 2 * i)
                            V.tensor_tensor(FG[b][:], HS[b][:], G[m % 4][:], MUL).then_inc(evac[m % 4], 1)
                            dve.wait_ge(S("fhi_ready"), F2 + k + 1 + 2 * i)
                            V.scalar_tensor_tensor(FLO[ch % 2][:, b + 2 * i, :], FG[b][:], 0.5,
                                                   f(FHI[ch % 2][:, b + 2 * i, :]), MUL, SUB).then_inc(S("hlo_ready"), 1)

        gate_up("fup0", 0)
        gate_up("fup1", 1)
        run("fdown0", add_to_x)
        gate_up("fup2", 2)
        run("fdown1", add_to_x)
        s0, _, b0, _ = PH["fdown2"]
        for j in range(4):
            if j < 3:
                split_lo(s0 + j + 1, (s0 + j + 1) % 2)
            for b in range(2):
                add_to_x(2 * j + b, b0 + 2 * j + b, 0)
        invert(8, (S("hs_ready"), 4 * KT))
        for k in range(KT):
            if k >= 2:
                dve.wait_ge(S("out_T"), k - 1)
            V.scalar_tensor_tensor(HS[k % 2][:], XT[:, k, :], col("norm_final_2", k), RSTD[:], MUL, MUL).then_inc(S("hs_ready"), 1)

    @block.gpsimd
    def _(pool):
        Q = nc.gpsimd
        Q.memset(VP[:, :, 0:30], 0.0).then_inc(S("pads_ready"), 1)
        gstep = Count(S("gpsimd_step"))

        def split_lo(s):
            pool.wait_ge(S("hi_done"), s + 1)
            if s:
                pool.wait_ge(S("lo_done"), s)
            Q.tensor_tensor(WLO[s % 2][:], RAW[s % 2][:], f(WHI[s % 2][:]), SUB).then_inc(S("lo_done"), 1)

        def window_sum(g):
            pool.wait_ge(*evac_at(2 * CC + g))
            src = UP[g % 2]
            for l in range(g + 1):
                sh, lo = 1 << l, (2 << l) - 1
                dst = S2[l % 2]
                if l:
                    gstep.wait(pool)
                elif g:
                    pool.wait_ge(S("pooled_ready"), g)
                ins = Q.tensor_tensor(dst[:, lo:16 + T], src[:, lo:16 + T], src[:, lo - sh:16 + T - sh], ADD)
                if l < g:
                    gstep.inc(ins)
                else:
                    ins.then_inc(S("window_summed"), 1)
                src = dst

        split_lo(0)
        pool.wait_ge(S("hlo_ready"), KT)
        for i in range(2):
            Q.memset(UP[i][:, 0:16], 0.0).then_inc(S("pads_ready"), 1)
        for s in range(1, 6):
            split_lo(s)
        pool.wait_ge(S("consts_loaded"), CONST_DMAS * 16)
        window_sum(0)
        window_sum(1)
        split_lo(6)
        window_sum(2)
        split_lo(7)
        window_sum(3)
        for s in range(8, 15):
            split_lo(s)
        def merge_sum(name, base, lo_base):
            s0, n, b0, bps = PH[name]
            with pool.Fori(0, n // 2) as i:
                for k in range(4):
                    m = b0 + 2 * k + 1
                    pool.wait_ge(*evac_at(m, i, 8))
                    pool.wait_ge(*evac_at(m - 1, i, 8))
                    pool.wait_ge(S("hlo_ready"), lo_base + k - 1 + 4 * i)
                    Q.tensor_tensor(HS[k % 2][:], GT[:, k + 4 * i, :], GT[:, KT + k + 4 * i, :], ADD).then_inc(S("merged_ready"), 1)

        merge_sum("branch", 0, KT)
        def add_squares(n, mean_at, ready):
            pool.wait_ge(S("mean_ready"), mean_at)
            Q.memset(SQA[:], 0.0).then_inc(S("sq_added"), 1)
            for j in range(KT - 1):
                pool.wait_ge(*ready(j))
                pool.wait_ge(S("sq_added"), KT * n + 1 + j)
                Q.tensor_tensor(SQA[:], SQA[:], SQ[j % 2][:], ADD).then_inc(S("sq_added"), 1)

        b0 = PH["wo"][2]
        add_squares(0, 1, lambda j: evac_at(b0 + j))
        add_squares(1, 3, lambda j: (S("ysq_ready"), j + 1))
        pool.wait_ge(S("block_full"), PH["small"][2])
        for i, n in enumerate(("cmp_k_w1_2", "cmp_v_w1_2")):
            pool.dma_start(W1[i][:], a[n][0].rearrange("(j p) h -> p j h", p=P)).then_inc(S("cmp_loaded"), 16)
        pool.dma_start(LEV32[:], a["c_level"].rearrange("p (l t) -> p l t", t=P)).then_inc(S("gla_consts"), 16)
        pool.dma_start(RESET[:], a["c_reset"]).then_inc(S("gla_consts"), 16)
        pool.dma_start(SIN[:], a["c_sin"]).then_inc(S("rope_loaded"), 16)
        pool.wait_ge(S("gla_consts"), 32)
        Q.tensor_copy(LEVM[:], LEV32[:]).then_inc(S("masks_small"), 1)
        Q.memset(ONEB[:], 1.0).then_inc(S("ones_ready"), 1)
        Q.memset(A[:], 0.0).then_inc(S("attn_zero"), 1)
        pool.wait_ge(S("mean_ready"), 5)
        pool.dma_start(COS[:], a["c_cos"]).then_inc(S("rope_loaded"), 16)

        def decayed_k(l, at_):
            for j in range(2):
                pool.wait_ge(S("decay_ready"), at_ + j + 1)
                if l:
                    pool.wait_ge(S("level_full"), 4 * l)
                Q.tensor_tensor(KL[:, j, :], KG[:, j, :], SQ[j][:], MUL).then_inc(S("kl_ready"), 1)

        for l in range(LEVELS + 1):
            decayed_k(l, 2 * l)
        pool.wait_ge(S("gla_out_full"), GLA_H)
        for i, n in enumerate(("cmp_k_w2_2", "cmp_v_w2_2")):
            pool.dma_start(W2[i][:], a[n][0]).then_inc(S("cmp_loaded"), 16)
        pool.wait_ge(S("rope_loaded"), 32)
        for n in range(6):
            x = KR[:, n, :] if n < 2 else QR[:, n - 2, :]
            pool.wait_ge(S("rotated"), n + 1)
            if n >= 2:
                pool.wait_ge(S("ropes_ready"), n - 1)
            Q.tensor_tensor(HS[n % 2][:], x, COS[:], MUL).then_inc(S("cos_ready"), 1)
        pool.wait_ge(S("ob_lo_ready"), GLA_H)
        for kv, name in enumerate(("cmp_pe_k_2", "cmp_pe_v_2")):
            Q.tensor_copy(Z[:, 2 * kv:2 * kv + 2, T:T + 32:2],
                          PV[:, ROW0[name]:ROW0[name] + 16].unsqueeze(1).broadcast_to([P, 2, 16])).then_inc(S("positions"), 1)
        pool.wait_ge(S("windows_a"), 4)
        pool.wait_ge(S("windows_b"), 4)
        Q.memset(VBD[:], 0.0).then_inc(S("blocks_zero"), 1)
        Q.memset(OTMP[:], 0.0).then_inc(S("oa_added"), 1)
        sM = PH["merge_a"][0]
        with pool.Fori(0, 2) as i:
            for t in range(TT):
                if t % 2 == 0:
                    s = sM + t // 2 + 1
                    pool.wait_ge(S("hi_done"), s + 1 + 2 * i)
                    pool.wait_ge(S("lo_done"), s + 2 * i)
                    Q.tensor_tensor(WLO[s % 2][:], RAW[s % 2][:], f(WHI[s % 2][:]), SUB).then_inc(S("lo_done"), 1)
                pool.wait_ge(read[3], 17 + t + 1 + 4 * i)
                Q.tensor_tensor(OA[:, t, :], OA[:, t, :], OTMP[:], ADD).then_inc(S("oa_added"), 1)
        merge_sum("branch2", KT, H2 + KT)
        add_squares(2, 5, lambda j: (S("ysq_ready"), KT + j + 1))
        add_squares(3, 6, lambda j: (S("ysq_ready"), 2 * KT + j + 1))


    ctx.close()


_CONSTS = constants()
_OUT = (1, T, D)


def kernel(**inputs):
    import concourse.bacc as _bacc
    from concourse import mybir as _mybir
    from concourse.bass_utils import run_bass_kernel_spmd as _run

    nc = _bacc.Bacc("TRN2", target_bir_lowering=False, num_devices=1)
    arrays = {name: np.ascontiguousarray(v) for name, v in inputs.items()}
    arrays["rows"] = np.concatenate([np.asarray(inputs[name]).reshape(-1, P) for name, _ in ROWS])
    arrays.update(_CONSTS)
    aps = {}
    for name, v in arrays.items():
        aps[name] = nc.dram_tensor(f"in_{name}", v.shape, _mybir.dt.from_np(v.dtype), kind="ExternalInput").ap()
    out = nc.dram_tensor("out", _OUT, _mybir.dt.float32, kind="ExternalOutput").ap()
    build(nc, aps, out)
    r = _run(nc, [{f"in_{name}": v for name, v in arrays.items()}], core_ids=[0])
    return r.results[0]["out"]
```
